# Optimizing a Trainium2 kernel written in Bass

```python
import math
import jax, jax.numpy as jnp
from jax import lax
import numpy as np

D_MODEL = 1024
BATCH = 1
SEQ = 512
DEPTH = 2

SSM_WIDTH = D_MODEL // 2
SSM_GROUP = 16
SSM_GROUPS = SSM_WIDTH // SSM_GROUP
SSM_STATE = 64
POOL_WIDTH = D_MODEL // 2
POOL_WINDOWS = (2, 4, 8, 16)
POOL_GROUP = POOL_WIDTH // len(POOL_WINDOWS)
HEAD_DIM = 64
N_HEADS = (D_MODEL // 2) // HEAD_DIM
N_KV_HEADS = 2
GQA_GROUP = N_HEADS // N_KV_HEADS
ATTN_WIDTH = N_HEADS * HEAD_DIM
KV_WIDTH = N_KV_HEADS * HEAD_DIM
BRANCH_WIDTH = D_MODEL // 2
N_BRANCH = 3
CMP_BLOCK = 32
CMP_STRIDE = 16
CMP_HIDDEN = 256
SEL_BLOCK = 64
SEL_TOP = 16
WINDOW = 512
Q_BLOCK = 64
ROPE_THETA = 10000.0
FF_HIDDEN = -(-8 * D_MODEL // (3 * 256)) * 256
DEEPNORM_ALPHA = (2 * DEPTH) ** 0.25
DEEPNORM_BETA = (8 * DEPTH) ** -0.25
LN_EPS = 1e-5
NEG = -1e30
IN_SIZES = (SSM_WIDTH, POOL_WIDTH, ATTN_WIDTH) + (KV_WIDTH,) * 6 + (3 * N_HEADS, N_BRANCH * D_MODEL)
IN_WIDTH = sum(IN_SIZES)
IN_OFFSETS = tuple(sum(IN_SIZES[:i + 1]) for i in range(len(IN_SIZES) - 1))

kernel_name = 'hybrid_s5_pool_nsa_deepnorm'

def layer_norm(x, g, b):
    xf = x.astype(jnp.float32)
    mu = jnp.mean(xf, -1, keepdims=True)
    var = jnp.mean(jnp.square(xf - mu), -1, keepdims=True)
    return ((xf - mu) * lax.rsqrt(var + LN_EPS) * g + b).astype(x.dtype)

def rope(x, positions):
    inv = ROPE_THETA ** (-jnp.arange(0, HEAD_DIM, 2, dtype=jnp.float32) / HEAD_DIM)
    ang = positions.astype(jnp.float32)[..., None] * inv
    cos = jnp.cos(ang)[:, :, None, :]
    sin = jnp.sin(ang)[:, :, None, :]
    x1, x2 = jnp.split(x.astype(jnp.float32), 2, axis=-1)
    return jnp.concatenate([x1 * cos - x2 * sin, x1 * sin + x2 * cos], -1).astype(x.dtype)

def masked_softmax(s, mask):
    s = jnp.where(mask, s.astype(jnp.float32), NEG)
    return jax.nn.softmax(s, axis=-1) * mask

def s5_mixer(u, a_re, a_im, log_dt, b_re, b_im, c_re, c_im, d_skip, w_glu):
    bsz, s, _ = u.shape
    f32 = jnp.float32
    uf = u.astype(f32).reshape(bsz, s, SSM_GROUPS, SSM_GROUP)
    lam = lax.complex(a_re.astype(f32), a_im.astype(f32))
    dt = jnp.exp(log_dt.astype(f32))[:, None]
    lam_bar = jnp.exp(lam * dt)
    b_bar = ((lam_bar - 1.0) / lam)[..., None] * lax.complex(b_re.astype(f32), b_im.astype(f32))
    bu = jnp.einsum('bsgc,gpc->bsgp', uf, b_bar)
    a = jnp.broadcast_to(lam_bar, bu.shape)

    def combine(left, right):
        a1, b1 = left
        a2, b2 = right
        return a1 * a2, a2 * b1 + b2

    _, h = lax.associative_scan(combine, (a, bu), axis=1)
    c = lax.complex(c_re.astype(f32), c_im.astype(f32))
    y = jnp.einsum('bsgp,gcp->bsgc', h, c).real + d_skip.astype(f32).reshape(SSM_GROUPS, SSM_GROUP) * uf
    y = jax.nn.gelu(y.reshape(bsz, s, SSM_WIDTH)).astype(u.dtype)
    val, gate = jnp.split(y @ w_glu, 2, axis=-1)
    return val * jax.nn.sigmoid(gate)

def pool_mixer(u, w_pool, pool_scale):
    bsz, s, _ = u.shape
    uf = u.astype(jnp.float32)
    csum = jnp.pad(jnp.cumsum(uf, axis=1), ((0, 0), (1, 0), (0, 0)))
    t = jnp.arange(s)
    outs = []
    for gi, w in enumerate(POOL_WINDOWS):
        sl = slice(gi * POOL_GROUP, (gi + 1) * POOL_GROUP)
        lo = jnp.maximum(t + 1 - w, 0)
        cnt = (t + 1 - lo).astype(jnp.float32)[None, :, None]
        mean = (csum[:, 1:, sl] - csum[:, lo, sl]) / cnt
        outs.append(mean - uf[:, :, sl])
    pooled = jnp.stack(outs, axis=2).astype(u.dtype)
    mixed = jnp.einsum('bsgc,gcd->bsgd', pooled, w_pool).reshape(bsz, s, POOL_WIDTH)
    return mixed * pool_scale

def nsa_mixer(q, k_cmp, v_cmp, k_sel, v_sel, k_win, v_win, gates, positions, cmp_pos, cmp_w1, cmp_b1, cmp_w2):
    bsz, s, _ = q.shape
    f32 = jnp.float32
    scale = HEAD_DIM ** -0.5
    t = jnp.arange(s)
    heads = lambda z: z.reshape(bsz, s, N_KV_HEADS, HEAD_DIM)
    q = rope(q.reshape(bsz, s, N_HEADS, HEAD_DIM), positions)
    qg = q.reshape(bsz, s, N_KV_HEADS, GQA_GROUP, HEAD_DIM)
    k_cmp = rope(heads(k_cmp), positions)
    v_cmp = heads(v_cmp)
    k_sel = rope(heads(k_sel), positions)
    v_sel = heads(v_sel)
    k_win = rope(heads(k_win), positions)
    v_win = heads(v_win)

    n_cmp = (s - CMP_BLOCK) // CMP_STRIDE + 1
    starts = jnp.arange(n_cmp) * CMP_STRIDE
    blk_idx = starts[:, None] + jnp.arange(CMP_BLOCK)[None, :]

    def compress(z, j):
        zb = z[:, blk_idx] + cmp_pos[j][None, None, :, None, :]
        zb = zb.transpose(0, 1, 3, 2, 4).reshape(bsz, n_cmp, N_KV_HEADS, CMP_BLOCK * HEAD_DIM)
        return jax.nn.gelu(zb @ cmp_w1[j] + cmp_b1[j]) @ cmp_w2[j]

    kc = compress(k_cmp, 0)
    vc = compress(v_cmp, 1)
    s_cmp = jnp.einsum('bshgd,bnhd->bhgsn', qg, kc, preferred_element_type=f32) * scale
    cmp_mask = (starts + CMP_BLOCK - 1)[None, :] <= t[:, None]
    p_cmp = masked_softmax(s_cmp, cmp_mask)
    o_cmp = jnp.einsum('bhgsn,bnhd->bshgd', p_cmp.astype(vc.dtype), vc)

    n_sel = s // SEL_BLOCK
    n_top = min(SEL_TOP, n_sel)
    sel_starts = jnp.arange(n_sel) * SEL_BLOCK
    overlap = jnp.clip(jnp.minimum(starts[:, None] + CMP_BLOCK, sel_starts[None, :] + SEL_BLOCK)
                       - jnp.maximum(starts[:, None], sel_starts[None, :]), 0).astype(f32) / CMP_BLOCK
    imp = jnp.einsum('bhgsn,nj->bhsj', p_cmp, overlap)
    cur = t // SEL_BLOCK
    jb = jnp.arange(n_sel)[None, :]
    forced = (jb == 0) | (jb == cur[:, None]) | (jb == cur[:, None] - 1)
    causal = sel_starts[None, :] <= t[:, None]
    score = jnp.where(forced, 1e30, jnp.where(causal, imp, NEG))
    top_val, top_idx = lax.top_k(score, n_top)
    top_ok = top_val > -1e29

    ks_blocks = k_sel.reshape(bsz, n_sel, SEL_BLOCK, N_KV_HEADS, HEAD_DIM).transpose(0, 3, 1, 2, 4)
    vs_blocks = v_sel.reshape(bsz, n_sel, SEL_BLOCK, N_KV_HEADS, HEAD_DIM).transpose(0, 3, 1, 2, 4)
    k_pad = jnp.pad(k_win, ((0, 0), (WINDOW, 0), (0, 0), (0, 0)))
    v_pad = jnp.pad(v_win, ((0, 0), (WINDOW, 0), (0, 0), (0, 0)))
    b_ix = jnp.arange(bsz)[:, None, None, None]
    h_ix = jnp.arange(N_KV_HEADS)[None, :, None, None]
    n_keys = n_top * SEL_BLOCK

    def query_block(i):
        s0 = i * Q_BLOCK
        tq = s0 + jnp.arange(Q_BLOCK)
        qb = lax.dynamic_slice_in_dim(qg, s0, Q_BLOCK, axis=1)
        idx = lax.dynamic_slice_in_dim(top_idx, s0, Q_BLOCK, axis=2)
        ok = lax.dynamic_slice_in_dim(top_ok, s0, Q_BLOCK, axis=2)
        kg = ks_blocks[b_ix, h_ix, idx].reshape(bsz, N_KV_HEADS, Q_BLOCK, n_keys, HEAD_DIM)
        vg = vs_blocks[b_ix, h_ix, idx].reshape(bsz, N_KV_HEADS, Q_BLOCK, n_keys, HEAD_DIM)
        key_pos = idx[..., None] * SEL_BLOCK + jnp.arange(SEL_BLOCK)
        m_sel = (ok[..., None] & (key_pos <= tq[None, None, :, None, None])).reshape(bsz, N_KV_HEADS, 1, Q_BLOCK, n_keys)
        sc = jnp.einsum('bqhgd,bhqkd->bhgqk', qb, kg, preferred_element_type=f32) * scale
        p = masked_softmax(sc, m_sel)
        o_sel = jnp.einsum('bhgqk,bhqkd->bqhgd', p.astype(vg.dtype), vg)
        kw = lax.dynamic_slice_in_dim(k_pad, s0, WINDOW + Q_BLOCK, axis=1)
        vw = lax.dynamic_slice_in_dim(v_pad, s0, WINDOW + Q_BLOCK, axis=1)
        kpos = s0 - WINDOW + jnp.arange(WINDOW + Q_BLOCK)
        diff = tq[:, None] - kpos[None, :]
        m_win = (kpos[None, :] >= 0) & (diff >= 0) & (diff < WINDOW)
        sc = jnp.einsum('bqhgd,bkhd->bhgqk', qb, kw, preferred_element_type=f32) * scale
        p = masked_softmax(sc, m_win)
        o_win = jnp.einsum('bhgqk,bkhd->bqhgd', p.astype(vw.dtype), vw)
        return o_sel, o_win

    o_sel, o_win = lax.map(query_block, jnp.arange(s // Q_BLOCK))
    o_sel = o_sel.transpose(1, 0, 2, 3, 4, 5).reshape(bsz, s, N_KV_HEADS, GQA_GROUP, HEAD_DIM)
    o_win = o_win.transpose(1, 0, 2, 3, 4, 5).reshape(bsz, s, N_KV_HEADS, GQA_GROUP, HEAD_DIM)
    g = jax.nn.sigmoid(gates.reshape(bsz, s, 3, N_KV_HEADS, GQA_GROUP, 1))
    out = g[:, :, 0] * o_cmp + g[:, :, 1] * o_sel + g[:, :, 2] * o_win
    return out.reshape(bsz, s, ATTN_WIDTH)

def setup_inputs(seed: int = 0) -> dict:
    key = jax.random.key(seed)
    ks = jax.random.split(key, 24)
    f32 = jnp.float32
    nrm = lambda k, shape, fan_in: jax.random.normal(k, shape, f32) * fan_in ** -0.5
    x = jax.random.normal(ks[0], (BATCH, SEQ, D_MODEL), f32)
    offsets = jax.random.randint(ks[1], (BATCH, 1), 0, 4096, dtype=jnp.int32)
    positions = offsets + jnp.arange(SEQ, dtype=jnp.int32)[None, :]
    w_in = nrm(ks[2], (DEPTH, D_MODEL, IN_WIDTH), D_MODEL)
    ssm_a_re = -0.5 + 0.01 * jax.random.normal(ks[3], (DEPTH, SSM_GROUPS, SSM_STATE), f32)
    ssm_a_im = math.pi * jnp.arange(SSM_STATE, dtype=f32) + 0.01 * jax.random.normal(ks[4], (DEPTH, SSM_GROUPS, SSM_STATE), f32)
    ssm_log_dt = jax.random.uniform(ks[5], (DEPTH, SSM_GROUPS), f32, math.log(1e-3), math.log(1e-1))
    ssm_b_re = nrm(ks[6], (DEPTH, SSM_GROUPS, SSM_STATE, SSM_GROUP), 2 * SSM_GROUP)
    ssm_b_im = nrm(ks[7], (DEPTH, SSM_GROUPS, SSM_STATE, SSM_GROUP), 2 * SSM_GROUP)
    ssm_c_re = nrm(ks[8], (DEPTH, SSM_GROUPS, SSM_GROUP, SSM_STATE), SSM_STATE)
    ssm_c_im = nrm(ks[9], (DEPTH, SSM_GROUPS, SSM_GROUP, SSM_STATE), SSM_STATE)
    ssm_d = jax.random.normal(ks[10], (DEPTH, SSM_WIDTH), f32)
    ssm_w_glu = nrm(ks[11], (DEPTH, SSM_WIDTH, 2 * SSM_WIDTH), SSM_WIDTH)
    pool_w = nrm(ks[12], (DEPTH, len(POOL_WINDOWS), POOL_GROUP, POOL_GROUP), POOL_GROUP)
    pool_scale = 1.0 + 0.02 * jax.random.normal(ks[13], (DEPTH, POOL_WIDTH), f32)
    cmp_pos = 0.02 * jax.random.normal(ks[14], (DEPTH, 2, CMP_BLOCK, HEAD_DIM), f32)
    cmp_w1 = nrm(ks[15], (DEPTH, 2, CMP_BLOCK * HEAD_DIM, CMP_HIDDEN), CMP_BLOCK * HEAD_DIM)
    cmp_b1 = 0.01 * jax.random.normal(ks[16], (DEPTH, 2, CMP_HIDDEN), f32)
    cmp_w2 = nrm(ks[17], (DEPTH, 2, CMP_HIDDEN, HEAD_DIM), CMP_HIDDEN)
    w_branch = nrm(ks[18], (DEPTH, N_BRANCH, BRANCH_WIDTH, D_MODEL), BRANCH_WIDTH)
    w_out = nrm(ks[19], (DEPTH, D_MODEL, D_MODEL), D_MODEL) * DEEPNORM_BETA
    ln_g = 1.0 + 0.02 * jax.random.normal(ks[20], (DEPTH, 2, D_MODEL), f32)
    ln_b = 0.02 * jax.random.normal(ks[21], (DEPTH, 2, D_MODEL), f32)
    ffn_w_in = nrm(ks[22], (DEPTH, D_MODEL, 2 * FF_HIDDEN), D_MODEL)
    ffn_w_out = nrm(ks[23], (DEPTH, FF_HIDDEN, D_MODEL), FF_HIDDEN) * DEEPNORM_BETA
    return {'x': x, 'positions': positions, 'w_in': w_in,
            'ssm_a_re': ssm_a_re, 'ssm_a_im': ssm_a_im, 'ssm_log_dt': ssm_log_dt,
            'ssm_b_re': ssm_b_re, 'ssm_b_im': ssm_b_im, 'ssm_c_re': ssm_c_re, 'ssm_c_im': ssm_c_im,
            'ssm_d': ssm_d, 'ssm_w_glu': ssm_w_glu, 'pool_w': pool_w, 'pool_scale': pool_scale,
            'cmp_pos': cmp_pos, 'cmp_w1': cmp_w1, 'cmp_b1': cmp_b1, 'cmp_w2': cmp_w2,
            'w_branch': w_branch, 'w_out': w_out, 'ln_g': ln_g, 'ln_b': ln_b,
            'ffn_w_in': ffn_w_in, 'ffn_w_out': ffn_w_out}

def reference(x, positions, w_in, ssm_a_re, ssm_a_im, ssm_log_dt, ssm_b_re, ssm_b_im, ssm_c_re, ssm_c_im,
              ssm_d, ssm_w_glu, pool_w, pool_scale, cmp_pos, cmp_w1, cmp_b1, cmp_w2,
              w_branch, w_out, ln_g, ln_b, ffn_w_in, ffn_w_out):
    bsz, s, _ = x.shape
    for l in range(DEPTH):
        proj = x @ w_in[l]
        (u_ssm, u_pool, q, k_c, v_c, k_s, v_s, k_w, v_w, nsa_g, br_g) = jnp.split(proj, IN_OFFSETS, axis=-1)
        y_ssm = s5_mixer(u_ssm, ssm_a_re[l], ssm_a_im[l], ssm_log_dt[l], ssm_b_re[l], ssm_b_im[l],
                         ssm_c_re[l], ssm_c_im[l], ssm_d[l], ssm_w_glu[l])
        y_pool = pool_mixer(u_pool, pool_w[l], pool_scale[l])
        y_nsa = nsa_mixer(q, k_c, v_c, k_s, v_s, k_w, v_w, nsa_g, positions,
                          cmp_pos[l], cmp_w1[l], cmp_b1[l], cmp_w2[l])
        branches = jnp.stack([y_ssm, y_pool, y_nsa], axis=2)
        branch_d = jnp.einsum('bskc,kcd->bskd', branches, w_branch[l])
        gate = jax.nn.sigmoid(br_g.reshape(bsz, s, N_BRANCH, D_MODEL))
        merged = jnp.sum(gate * branch_d, axis=2)
        x = layer_norm(DEEPNORM_ALPHA * x + merged @ w_out[l], ln_g[l, 0], ln_b[l, 0])
        h_gate, h_up = jnp.split(x @ ffn_w_in[l], 2, axis=-1)
        x = layer_norm(DEEPNORM_ALPHA * x + (jax.nn.silu(h_gate) * h_up) @ ffn_w_out[l], ln_g[l, 1], ln_b[l, 1])
    return x


_drawn_inputs = setup_inputs


def setup_inputs(seed=0):
    import zlib

    import numpy as np

    out = dict(_drawn_inputs(seed))
    spreads = {}
    factors = {'ssm_a_re': 64.0,
     'ssm_a_im': 51.096,
     'ssm_log_dt': 52.36,
     'ssm_b_re': 64.0,
     'ssm_b_im': 64.0,
     'ssm_c_re': 64.0,
     'ssm_c_im': 64.0,
     'pool_scale': 8.0,
     'cmp_pos': 54.742,
     'cmp_b1': 64.0,
     'cmp_w1': 2.773}
    for name, (base, spread) in spreads.items():
        noise = np.random.default_rng([zlib.crc32(name.encode()), seed]).standard_normal(out[name].shape)
        drawn = base * np.exp(spread * noise) if base else spread * noise
        out[name] = __import__('jax').numpy.asarray(drawn.astype(out[name].dtype))
    for name, factor in factors.items():
        out[name] = (out[name] * factor).astype(out[name].dtype)
    return out
```

```python
import math
from contextlib import ExitStack

import numpy as np

import concourse.bass as bass
from concourse import mybir

D, S, L, P = 1024, 512, 2, 128
KD = D // P
FF = 2816
KF = FF // P
HD, CH, NCMP, CSTR = 64, 256, 31, 16
SG, SC, SN = 32, 16, 64
TAP, NCH = 8, S // 8
GP = SG // 2
ALPHA = (2 * L) ** 0.25
EPS = 1e-5
NEG = -1e30
SCALE = HD ** -0.5
GELU_A, GELU_B = 0.044715, math.sqrt(2.0 / math.pi)
MAGIC = 12582912.0
TWO_PI_1 = 6.28125
TWO_PI_2 = 0.00193500518798828125
TWO_PI_3 = 2 * math.pi - TWO_PI_1 - TWO_PI_2
PI_F = 3.1415925

NA1, NA2, NB1, NB2, NGL, NC, NO, NF, NG = 6, 4, 2, 4, 4, 10, 8, 44, 24
OA1 = 0
OA2 = OA1 + NA1
OB1 = OA2 + NA2
OB2 = OB1 + 4 * NB1
OGL = OB2 + 4 * NB2
OC = OGL + NGL
OO = OC + 2 * NC
OF = OO + NO
OG = OF + NF
NSLAB = OG + NG
ACT_OUTS = OGL
DGL, DC, DO, DF = 0, 8, 40, 48
DG = DF + 44
DVE_OUTS = DG + 8

SM = {}
_at = 0
for _n, _w in (("are", GP), ("aim", GP), ("ldt", GP), ("bre", GP * SC), ("bim", GP * SC), ("cre", GP * SC),
               ("cim", GP * SC), ("dsk", SG), ("psc", 4), ("b1", 4), ("wg", KD * 24), ("wpool", 4 * P),
               ("w2", 4 * HD), ("pos", 2 * SC)):
    SM[_n] = (_at, _at + _w)
    _at += _w
NSM = _at
CN = {}
_at = 0
for _n, _w in (("ident", P), ("rot", P), ("dmask", P), ("cadd", 4 * NCMP), ("c01", 4 * NCMP), ("icnt", 64), ("inv", 1)):
    CN[_n] = (_at, _at + _w)
    _at += _w
NCN = _at


def build_program(nc, wstream, w1s, smalls, norms, consts, xin, pos, out):
    f32, f32r, i32 = mybir.dt.float32, mybir.dt.float32r, mybir.dt.int32
    ACT = mybir.ActivationFunctionType
    ALU = mybir.AluOpType
    AX = mybir.AxisListType
    ds = bass.ds
    ADD, SUB, MUL, MAX, MIN = ALU.add, ALU.subtract, ALU.mult, ALU.max, ALU.min

    scr_u = nc.dram_tensor("scratch_u", (SC, 8, TAP, NCH), f32).ap()
    scr_y = nc.dram_tensor("scratch_y", (SC, TAP, 8, NCH), f32).ap()
    scr_k = nc.dram_tensor("scratch_k", (SC, 8, 2 * P), f32).ap()

    base = -(-nc.sbuf_base // 32) * 32
    used = {}

    def place(name, at, shape, dt=f32):
        n = 1
        for d in shape[1:]:
            n *= d
        used[name] = (at, at + n)
        return nc.alloc_sbuf_tensor_at(name, shape, dt, offset=base + 4 * at)

    top = [0]

    def own(name, shape, dt=f32):
        n = 1
        for d in shape[1:]:
            n *= d
        n = -(-n // 8) * 8
        t = place(name, top[0], shape, dt)
        top[0] += n
        return t

    xf_at = top[0]
    xf = own("xf", [P, KD, S])
    xh = own("xh", [P, KD, S], f32r)
    xl = own("xl", [P, KD, S], f32r)
    raw = own("raw", [P, 2, 1024])
    whi = own("whi", [P, 2, 1024], f32r)
    wlo = own("wlo", [P, 2, 1024], f32r)
    big_at = top[0]
    top[0] += 2 * KF * S
    hh = place("hh", big_at, [P, KF, S], f32r)
    hl = place("hl", big_at + KF * S, [P, KF, S], f32r)
    gates = place("gates", big_at, [P, 16, S])
    r1 = place("r1", big_at, [P, KD, S])
    w1 = place("w1", big_at, [P, 2, 16 * CH])
    nsh = place("nsh", big_at + 8192, [P, 4, S], f32r)
    nsl = place("nsl", big_at + 10240, [P, 4, S], f32r)
    plh = place("plh", big_at + 12288, [P, 4, S], f32r)
    pll = place("pll", big_at + 14336, [P, 4, S], f32r)
    glh = place("glh", big_at + 16384, [P, 4, S], f32r)
    gll = place("gll", big_at + 18432, [P, 4, S], f32r)
    upool = place("upool", big_at + 20480, [P, 4, S])
    ys_at = top[0]
    ysh = own("ysh", [P, 4, S], f32r)
    ysl = own("ysl", [P, 4, S], f32r)
    mgh = place("mgh", ys_at, [P, KD, S], f32r)
    mgl = place("mgl", xf_at, [P, KD, S], f32r)
    cos_t = own("cos_t", [P, S])
    sin_t = own("sin_t", [P, S])
    kv_at = top[0]
    kro = own("kro", [P, 2, S])
    vtok = own("vtok", [P, 2, 4, P])
    toep = own("toep", [P, 8, P])
    sm = own("sm", [P, NSM])
    nrm = own("nrm", [P, L, 32])
    cn = own("cn", [P, NCN])
    kct = own("kct", [P, NCMP])
    vct = own("vct", [32, 2, HD])
    gq = own("gq", [P, 4, 24])
    tiny = own("tiny", [P, 64])
    carry = own("carry", [1, 8])
    pa = place("pa", big_at + 8192, [P, 10, S])
    at = big_at + 8192 + 10 * S

    def more(name, shape):
        nonlocal at
        t = place(name, at, shape)
        at += -(-int(np.prod(shape[1:])) // 8) * 8
        return t

    eph = more("eph", [P, 2, GP, NCH])
    r8m = more("r8m", [P, GP, NCH])
    lam = more("lam", [P, 2, 9, GP])
    php = more("php", [P, 2, 9, GP])
    coef = more("coef", [P, 2, GP])
    rp = more("rp", [P, 9, GP])
    st = more("st", [P, 16, GP])
    ubl = more("ubl", [P, TAP, NCH])
    hst = more("hst", [P, 2, 4, NCH + 1])
    bch = more("bch", [P, 2, 4, SC])
    ta = more("ta", [P, 576])
    tb = more("tb", [P, 576])
    assert at <= big_at + 20480, at - big_at
    at = big_at + 4096
    srot = more("srot", [P, 2, 4, NCH])
    gsc = more("gsc", [P, 2, 4, NCH])
    y8 = more("y8", [P, 8, NCH])
    assert at <= big_at + 6144
    yfm = place("yfm", big_at + 6144, [P, 4, S])
    ygt = place("ygt", xf_at, [P, S])
    at = xf_at
    vmat = more("vmat", [P, 2, 4, TAP * SC])
    vt = more("vt", [P, 2, 4, P])
    wmat = more("wmat", [P, 2, 4, 9 * SC])
    u8 = more("u8", [P, 8, NCH])
    assert at <= xf_at + 4096
    kam = place("kam", ys_at, [SC, 8, P])
    skip = place("skip", ys_at + 1024, [SC, 8, SC])
    at = xf_at
    zpm = more("zpm", [P, 2, 2, S // 2])
    z2 = more("z2", [P, 2, 2, S // 2])
    zb = more("zb", [P, 2, 16, 2, NCMP])
    assert at <= xf_at + 4096
    hid = place("hid", big_at + 20480, [P, 4, 2 * NCMP])
    hgt = place("hgt", big_at + 20480 + 256, [P, 4, 2 * NCMP])
    rt1 = place("rt1", big_at + 20480 + 512, [P, S])
    rt2 = place("rt2", big_at + 20480 + 1024, [P, S])
    at = big_at + 12288
    prob = more("prob", [P, 2, 2, S])
    probt = more("probt", [P, 2, 2, S])
    pct = more("pct", [32, 8, P])
    pc = more("pc", [P, 8, NCMP])
    qraw = more("qraw", [P, S])
    qro = more("qro", [P, S])
    qt1 = more("qt1", [P, S])
    qt2 = more("qt2", [P, S])
    assert at <= big_at + 20480
    pla = place("pla", xf_at, [P, 4, S])
    plb = place("plb", xf_at + 2048, [P, 4, S])
    gt = place("gt", kv_at, [P, S])
    gv = place("gv", kv_at + 512, [P, S])
    acc = place("acc", kv_at, [P, 2, S])
    tmp = place("tmp", kv_at + 1024, [P, 2, S])
    tg2 = place("tg2", big_at + 20480, [P, 2, S])
    lnbc = place("lnbc", kv_at, [P, 2, 4, P])
    lnst = place("lnst", kv_at + 1024, [P, 4, KD, 6])
    lnmv = place("lnmv", kv_at + 1024 + 192, [P, 4, 2])
    lnrs = place("lnrs", kv_at + 1024 + 200, [P, 4])
    rst = place("rst", ys_at, [P, 2, S])
    ft = place("ft", ys_at, [P, 2, S])
    fa = place("fa", ys_at + 1024, [P, 2, S])
    fb = place("fb", ys_at + 2048, [P, 2, S])

    ctx = ExitStack()
    with ctx:
        ps = ctx.enter_context(nc.psum_tensor("ps", [P, 8, S], f32))

        def sem(name):
            return ctx.enter_context(nc.semaphore(name))

        raw_loaded = [sem("raw_loaded_even"), sem("raw_loaded_odd")]
        hi_ready, lo_ready, slab_done = sem("hi_ready"), sem("lo_ready"), sem("slab_done")
        act_out_freed, dve_out_freed = sem("act_out_freed"), sem("dve_out_freed")
        x_in, x_hi, x_ready = sem("x_in"), sem("x_hi"), sem("x_ready")
        consts_in, small_in = sem("consts_in"), sem("small_in")
        w1_in = [sem("w1_keys_in"), sem("w1_values_in")]
        rope_arg, rope_done = sem("rope_arg"), sem("rope_done")
        toep_zero = sem("toep_zero")
        qgate_psum, qgate_tanh = sem("qgate_psum"), sem("qgate_tanh")
        krot_psum, krot_done = sem("krot_psum"), sem("krot_done")
        vtok_psum, vtok_ready = sem("vtok_psum"), sem("vtok_ready")
        z_perm, z_ready = sem("z_perm"), sem("z_ready")
        z2_in = [sem("z2_keys_in"), sem("z2_values_in")]
        hid_psum, hid_biased, hid_ready = sem("hid_psum"), sem("hid_biased"), sem("hid_ready")
        kc_psum, kc_ready = sem("kc_psum"), sem("kc_ready")
        gelu_arg, gelu_tanh = sem("gelu_arg"), sem("gelu_tanh")
        dt_ready, angle_ready, sincos_ready = (sem(n) for n in ("dt_ready", "angle_ready", "sincos_ready"))
        ubl_ready, u_stored, u8_in = sem("ubl_ready"), sem("u_stored"), sem("u8_in")
        mats_ready, vt_psum, vt_ready, ka_psum, ka_copied, ka_ready, k_stored, toep_in = (
            sem(n) for n in ("mats_ready", "vt_psum", "vt_ready", "ka_psum", "ka_copied", "ka_ready", "k_stored", "toep_in"))
        x_state_psum, h_ready, y_psum, y8_ready, y_stored, yfm_in = (sem(n) for n in ("x_state_psum", "h_ready", "y_psum", "y8_ready", "y_stored", "yfm_in"))
        ygelu_ready, ys_hi, ys_ready = sem("ygelu_ready"), sem("ys_hi"), sem("ys_ready")
        q_rot_psum, q_ready = sem("q_rot_psum"), sem("q_ready")
        cs_psum, cs_shift, cs_exp, cs_ready, cs_tpsum, cs_tready = (sem(n) for n in ("cs_psum", "cs_shift", "cs_exp", "cs_ready", "cs_tpsum", "cs_tready"))
        s_psum, s_max, s_exp, s_ready, s_tpsum, pt_sel, pt_win, o_psum, o_hi, o_ready = (
            sem(n) for n in ("s_psum", "s_max", "s_exp", "s_ready", "s_tpsum", "pt_sel", "pt_win", "o_psum", "o_hi", "o_ready"))
        pool_ready, mix_psum, mix_hi, mix_ready = sem("pool_ready"), sem("mix_psum"), sem("mix_hi"), sem("mix_ready")
        glu_tanh, glu_raw, glu_hi, glu_ready = sem("glu_tanh"), sem("glu_raw"), sem("glu_hi"), sem("glu_ready")
        mg_tanh, mg_raw, mg_hi, mg_ready = sem("mg_tanh"), sem("mg_raw"), sem("mg_hi"), sem("mg_ready")
        r_ready, rt_psum, stats_done, var_ready, sd_ready, ln_bc, ln_psum, ln_norm, ln_x = (
            sem(n) for n in ("r_ready", "rt_psum", "stats_done", "var_ready", "sd_ready", "ln_bc", "ln_psum", "ln_norm", "ln_x"))
        ff_tanh, ff_raw, ff_hi, ff_ready = sem("ff_tanh"), sem("ff_raw"), sem("ff_hi"), sem("ff_ready")
        r_kept, out_done = sem("r_kept"), sem("out_done")
        block = ctx.enter_context(nc.Block())

        def sbank(s):
            return 4 if s % 2 == 0 else 0

        def smv(name, *shape):
            a, b = SM[name]
            v = sm[:, a:b]
            if len(shape) == 2:
                v = v.rearrange("p (a b) -> p a b", a=shape[0])
            return v

        def cnv(name):
            a, b = CN[name]
            return cn[:, a:b]

        def bc(ap, axis, n):
            v = ap.unsqueeze(axis)
            shape = list(v.shape)
            shape[axis] = n
            return v.to_broadcast(shape)

        @block.sync
        def _(sp):
            with sp.Fori(0, L * NSLAB // 2) as h:
                for s in range(2):
                    sp.wait_ge(lo_ready, h * 2 + (s + 1))
                    sp.dma_start(raw[:, s, :], wstream[ds(h * 2 + s, 1), :, :].rearrange("a p n -> p (a n)"))\
                        .then_inc(raw_loaded[s], 16)
            sp.wait_ge(lo_ready, L * NSLAB + 1)
            sp.dma_start(raw[:, 0, :], wstream[L * NSLAB - 1, :, :]).then_inc(raw_loaded[0], 16)
            sp.wait_ge(x_ready, 4 + 8 * L)
            sp.dma_start(out, xf[:, :, :]).then_inc(out_done, 16)
            sp.wait_ge(out_done, 16)

        @block.gpsimd
        def _(pool):
            def wait(signal, value):
                pool.drain()
                pool.wait_ge(signal, value)
                pool.tensor_tensor(carry[:, 0:1], carry[:, 1:2], carry[:, 1:2], ADD)

            pool.dma_start(xf[:, :, :], xin).then_inc(x_in, 16)
            pool.dma_start(cn[:, :], consts).then_inc(consts_in, 16)
            pool.dma_start(nrm[:, :, :], norms).then_inc(consts_in, 16)
            pool.dma_start(kro[:, 0, :].bitcast(i32), pos.partition_broadcast(P)).then_inc(consts_in, 16)
            pool.memset(toep[:, :, :], 0.0).then_inc(toep_zero, 1)
            pool.memset(carry[:, :], 0.0).then_inc(toep_zero, 1)
            pool.wait_ge(toep_zero, 2)
            pool.dma_start(scr_k[:, :, 0:P], toep[0:SC, :, :]).then_inc(k_stored, 16)
            pool.wait_ge(k_stored, 16)
            with pool.Fori(0, L) as l:
                wait(mix_ready, l * 4 + 1)
                pool.dma_start(sm[:, :], smalls[ds(l, 1), :, :].rearrange("a p n -> p (a n)")).then_inc(small_in, 16)
                wait(dve_out_freed, l * DVE_OUTS + 4)
                for j in range(2):
                    pool.dma_start(w1[:, j, :], w1s[ds(l * 2 + j, 1), :, :].rearrange("a p n -> p (a n)")).then_inc(w1_in[j], 16)
                for j in range(2):
                    wait(z_perm, l * 2 + (j + 1))
                    for e in range(2):
                        for h in range(2):
                            pool.dma_start(z2[64 * e:64 * e + 64, j, h, :], zpm[64 * h:64 * h + 64, j, e, :]).then_inc(z2_in[j], 16)

                def store_u(b):
                    wait(ubl_ready, b + 1)
                    pool.dma_start(scr_u.rearrange("c g t n -> g c (t n)"), ubl[:, :, :].rearrange("p t n -> p (t n)")).then_inc(u_stored, 16)

                def load_u(b):
                    wait(u_stored, b * 16 + 16)
                    pool.dma_start(u8[:, :, :], scr_u.rearrange("c g t n -> t (c g) n")).then_inc(u8_in, 16)

                def build_toep(b):
                    wait(ka_ready, b + 1)
                    pool.dma_start(scr_k[:, :, P:2 * P], kam[:, :, :]).then_inc(k_stored, 16)
                    wait(k_stored, b * 16 + 32)
                    rows = scr_k.rearrange("c g x -> (c g) x")
                    src = bass.AP(tensor=rows.tensor, offset=SC, ap=[[SC, TAP], [2 * P, SC * 8], [1, P]])
                    pool.dma_start(toep[:, :, :], src).then_inc(toep_in, 16)

                def move_y(b, j):
                    wait(y8_ready, b + 2)
                    pool.dma_start(scr_y.rearrange("c t g n -> t c (g n)"), y8[:, :, :].rearrange("p g n -> p (g n)")).then_inc(y_stored, 16)
                    wait(y_stored, b * 16 + 16)
                    pool.dma_start(yfm[:, ds(j, 1), :].rearrange("p a (t n) -> p (a t) n", n=NCH), scr_y.rearrange("c t g n -> g (c t) n")).then_inc(yfm_in, 16)

                store_u(l * 4)
                load_u(l * 4)
                build_toep(l * 4)
                with pool.Fori(0, 3) as j:
                    b = l * 4 + j
                    store_u(b + 1)
                    move_y(b, j)
                    load_u(b + 1)
                    build_toep(b + 1)
                move_y(l * 4 + 3, 3)

        @block.tensor
        def _(pe):
            def products(bank, slot, blocks, hi, lo, first=True, last=True):
                for i, (blk, k) in enumerate(blocks):
                    wh = whi[:, slot, blk * P:blk * P + P]
                    wl = wlo[:, slot, blk * P:blk * P + P]
                    pe.matmul(ps[:, bank, :], wh, hi[:, k, :], start=first and i == 0, stop=False)
                    pe.matmul(ps[:, bank, :], wh, lo[:, k, :], start=False, stop=False)
                    m = pe.matmul(ps[:, bank, :], wl, hi[:, k, :], start=False, stop=last and i == len(blocks) - 1)
                return m

            all_k = [(k, k) for k in range(KD)]

            def x_slab(h, c, bank, freed, o):
                pe.wait_ge(lo_ready, h * 2 + (c + 3))
                pe.wait_ge(freed, o)
                products(bank, c % 2, all_k, xh, xl).then_inc(slab_done, 1)

            ident = cnv("ident")
            pe.wait_ge(consts_in, 48)
            with pe.Fori(0, L) as l:
                hl_ = l * (NSLAB // 2)
                ao = l * ACT_OUTS
                do = l * DVE_OUTS
                pe.wait_ge(x_ready, l * 8 + 4)
                pe.wait_ge(small_in, l * 16 + 16)
                pe.wait_ge(dve_out_freed, do + 4)
                wg = smv("wg", KD, 24)
                for t in range(4):
                    for k in range(KD):
                        m = pe.matmul(ps[:, 7, 24 * t:24 * t + 24], xf[:, k, P * t:P * t + P], wg[:, k, :],
                                      start=k == 0, stop=k == KD - 1)
                m.then_inc(qgate_psum, 1)
                with pe.Fori(0, NA1 // 2) as i:
                    for c in range(2):
                        x_slab(hl_ + i, c, c, act_out_freed, ao + i * 2 + (c + 1))
                for i in range(3):
                    pe.wait_ge(act_out_freed, ao + 2 + (i + 1))
                    pe.matmul(ps[:, 4 + i, :], cnv("rot"), pa[:, i, :], start=True, stop=True).then_inc(krot_psum, 1)
                pe.wait_ge(act_out_freed, ao + 2 + 6)
                for v in range(2):
                    for t in range(4):
                        m = pe.transpose(ps[:, 2 + v, P * t:P * t + P], pa[:, 4 + v, P * t:P * t + P], ident)
                    m.then_inc(vtok_psum, 1)
                def a2_slab(i):
                    x_slab(hl_ + (OA2 + i - i % 2) // 2, i % 2, i % 2, act_out_freed, ao + OA2 + (i + 1))

                a2_slab(0)
                a2_slab(1)
                for j in range(2):
                    pe.wait_ge(z_ready, l * 2 + (j + 1))
                    pe.wait_ge(w1_in[j], (l + 1) * 16)
                    if j == 0:
                        pe.wait_ge(krot_done, l * 3 + 3)
                    for m2 in range(2):
                        for t in range(16):
                            m = pe.matmul(ps[:, 4, (2 * j + m2) * 62:(2 * j + m2 + 1) * 62],
                                          w1[:, j, t * CH + m2 * P:t * CH + m2 * P + P],
                                          zb[:, j, t, :, :].rearrange("p h n -> p (h n)"), start=t == 0, stop=t == 15)
                m.then_inc(hid_psum, 1)
                a2_slab(2)
                pe.wait_ge(hid_ready, l + 1)
                w2 = smv("w2", 4, HD)
                for h in range(2):
                    for m2 in range(2):
                        pe.matmul(ps[64 * h:64 * h + 64, 5, 0:NCMP], w2[:, m2, :], hgt[:, m2, NCMP * h:NCMP * h + NCMP],
                                  start=m2 == 0, stop=m2 == 1)
                for h in range(2):
                    for m2 in range(2):
                        m = pe.matmul(ps[0:NCMP, 6, HD * h:HD * h + HD], hgt[:, 2 + m2, NCMP * h:NCMP * h + NCMP], w2[:, 2 + m2, :],
                                      start=m2 == 0, stop=m2 == 1)
                m.then_inc(kc_psum, 1)
                a2_slab(3)

                def s5_mats(b):
                    pe.wait_ge(mats_ready, b + 1)
                    for q in range(2):
                        for g in range(4):
                            m = pe.transpose(ps[:, 4 + q, P * g:P * g + P], vmat[:, q, g, :], ident)
                    m.then_inc(vt_psum, 1)
                    for par in range(2):
                        rows = slice(64 * par, 64 * par + 64)
                        for g in range(4):
                            for q in range(2):
                                m = pe.matmul(ps[0:SC, 2 + par, P * g:P * g + P], bch[rows, q, g, :], wmat[rows, q, g, 0:P],
                                              start=q == 0, stop=q == 1)
                    m.then_inc(ka_psum, 1)

                def s5_chunk(b, h, j):
                    pe.wait_ge(vt_ready, b + 1)
                    pe.wait_ge(u8_in, b * 16 + 16)
                    for q in range(2):
                        for g in range(8):
                            par, gp = g % 2, g // 2
                            m = pe.matmul(ps[64 * par:64 * par + 64, 4, (4 * q + gp) * NCH:(4 * q + gp + 1) * NCH],
                                          vt[:, q, gp, 64 * par:64 * par + 64], u8[:, g, :], start=True, stop=True)
                    m.then_inc(x_state_psum, 1)
                    x_slab(h, 0, 0, act_out_freed, ao + OB1 + j * 2 + 1)
                    pe.wait_ge(toep_in, b * 16 + 16)
                    pe.wait_ge(h_ready, b + 1)
                    pe.wait_ge(y8_ready, b + 1)
                    for par in range(2):
                        rows = slice(64 * par, 64 * par + 64)
                        for gp in range(4):
                            o = ps[:, 6 + par, gp * NCH:(gp + 1) * NCH]
                            pe.matmul(o, toep[:, 2 * gp + par, :], u8[:, 2 * gp + par, :], start=True, stop=False)
                            pe.matmul(o, wmat[rows, 0, gp, SC:9 * SC], hst[rows, 0, gp, 0:NCH], start=False, stop=False)
                            m = pe.matmul(o, wmat[rows, 1, gp, SC:9 * SC], hst[rows, 1, gp, 0:NCH], start=False, stop=True)
                    m.then_inc(y_psum, 1)
                    x_slab(h, 1, 1, act_out_freed, ao + OB1 + j * 2 + 2)

                pe.wait_ge(kc_ready, l + 1)
                pe.wait_ge(vtok_ready, l + 1)
                s5_mats(l * 4)
                with pe.Fori(0, 3) as j:
                    s5_chunk(l * 4 + j, hl_ + OB1 // 2 + j, j)
                    s5_mats(l * 4 + j + 1)
                s5_chunk(l * 4 + 3, hl_ + OB1 // 2 + 3, 3)
                with pe.Fori(0, 4) as j:
                    b = l * 4 + j
                    h = hl_ + OB2 // 2 + j * 2

                    def slab(c):
                        x_slab(h, c, c % 2, act_out_freed, ao + OB2 + j * 4 + (c + 1))

                    slab(0)
                    slab(1)
                    pe.wait_ge(act_out_freed, ao + OB2 + j * 4 + 3)
                    pe.wait_ge(y8_ready, l * 4 + 5)
                    pe.matmul(ps[:, 6, :], cnv("rot"), qraw[:, :], start=True, stop=True).then_inc(q_rot_psum, 1)
                    slab(2)
                    pe.wait_ge(q_ready, b + 2)
                    for kv in range(2):
                        rows = slice(64 * kv, 64 * kv + 64)
                        for t in range(4):
                            m = pe.matmul(ps[:, 4 + kv, NCMP * t:NCMP * t + NCMP], qro[rows, P * t:P * t + P], kct[rows, :],
                                          start=True, stop=True)
                    m.then_inc(cs_psum, 1)
                    slab(3)

                    def scores(s):
                        kv, t = s // 4, s % 4
                        rows = slice(64 * kv, 64 * kv + 64)
                        n = P * (t + 1)
                        for br in range(2):
                            m = pe.matmul(ps[:, sbank(s) + br, 0:n], qro[rows, P * t:P * t + P], kro[rows, br, 0:n], start=True, stop=True)
                        m.then_inc(s_psum, 1)

                    pe.wait_ge(cs_shift, b + 1)
                    scores(0)
                    pe.wait_ge(cs_ready, b + 1)
                    for i in range(8):
                        m = pe.transpose(ps[0:NCMP, 2 + i // 4, P * (i % 4):P * (i % 4) + P], pc[:, i, :], ident)
                    m.then_inc(cs_tpsum, 1)
                    pe.wait_ge(act_out_freed, ao + OB2 + j * 4 + 6)
                    scores(1)
                    pe.wait_ge(vtok_ready, l + 1)
                    for s in range(8):
                        kv, t = s // 4, s % 4
                        pe.wait_ge(s_ready, b * 8 + (s + 1))
                        if s == 0:
                            pe.wait_ge(cs_tready, b + 1)
                        for br in range(2):
                            for k in range(t + 1):
                                m = pe.transpose(ps[:, 2 + br, P * k:P * k + P], prob[:, s % 2, br, P * k:P * k + P], ident)
                        m.then_inc(s_tpsum, 1)
                        if s < 6:
                            scores(s + 2)
                        o = ps[64 * kv:64 * kv + 64, 7, P * t:P * t + P]
                        if s == 0:
                            pe.wait_ge(o_ready, b + 1)
                        pe.matmul(o, vct[0:NCMP, kv, :], pct[0:NCMP, s, :], start=True, stop=False)
                        for br, there in ((0, pt_sel), (1, pt_win)):
                            pe.wait_ge(there, b * 8 + (s + 1))
                            for k in range(t + 1):
                                m = pe.matmul(o, vtok[:, br, k, 64 * kv:64 * kv + 64], probt[:, s % 2, br, P * k:P * k + P],
                                              start=False, stop=br == 1 and k == t)
                        m.then_inc(o_psum, 1)
                wp = smv("wpool", 4, P)
                pe.wait_ge(pool_ready, l + 1)
                pe.wait_ge(o_ready, l * 4 + 5)
                for g in range(4):
                    src = (pla if g % 2 == 0 else plb)[:, g, :]
                    pe.matmul(ps[:, 4 + g, :], wp[:, g, :], src, start=True, stop=True).then_inc(mix_psum, 1)
                four = [(k, k) for k in range(4)]
                four_up = [(4 + k, k) for k in range(4)]
                with pe.Fori(0, NGL // 2) as i:
                    h = hl_ + OGL // 2 + i
                    pe.wait_ge(ys_ready, l * 4 + 4)
                    pe.wait_ge(act_out_freed, ao + ACT_OUTS + 2)
                    for c in range(2):
                        pe.wait_ge(lo_ready, h * 2 + (c + 3))
                        pe.wait_ge(dve_out_freed, do + DGL + i * 4 + (2 * c + 2))
                        products(2 * c, c, four, ysh, ysl)
                        products(2 * c + 1, c, four_up, ysh, ysl).then_inc(slab_done, 1)
                with pe.Fori(0, 2) as i:
                    pe.wait_ge(glu_ready, l * 4 + 4)
                    pe.wait_ge(mix_ready, l * 4 + 5)
                    for c in range(10):
                        q = c % 5
                        h = hl_ + OC // 2 + i * 5
                        first = do + DC + i * 16 + (8 * (c // 5))
                        bank = (0, 2, 0, 1, 2)[q]
                        if q in (2, 3):
                            x_slab(h, c, bank, dve_out_freed, first + (4 + (q - 2) + 1))
                            continue
                        pe.wait_ge(lo_ready, h * 2 + (c + 3))
                        pe.wait_ge(dve_out_freed, first + {0: 2, 1: 4, 4: 8}[q])
                        hi, lo = {0: (glh, gll), 1: (plh, pll), 4: (nsh, nsl)}[q]
                        products(bank, c % 2, four, hi, lo)
                        products(bank + 1, c % 2, four_up, hi, lo).then_inc(slab_done, 1)

                def to_tokens(rbuf, m, count):
                    pe.wait_ge(r_ready, count + 1)
                    pe.wait_ge(stats_done, count + 1)
                    for t in range(4):
                        x = pe.transpose(ps[:, 4 + m % 2, P * t:P * t + P], rbuf[:, m, P * t:P * t + P], ident)
                    x.then_inc(rt_psum, 1)

                def spread(n):
                    pe.wait_ge(ln_bc, n + 1)
                    for w in range(2):
                        for t in range(4):
                            x = pe.transpose(ps[:, 6 + w, P * t:P * t + P], lnbc[:, w, t, :], ident)
                    x.then_inc(ln_psum, 1)

                pe.wait_ge(mg_ready, l * 4 + 4)
                for c in range(NO):
                    pe.wait_ge(lo_ready, (hl_ + OO // 2) * 2 + (c + 3))
                    pe.wait_ge(dve_out_freed, do + DO + (c + 1))
                    products(c % 4, c % 2, all_k, mgh, mgl).then_inc(slab_done, 1)
                    if c:
                        to_tokens(r1, c - 1, l * 16 + (c - 1))
                to_tokens(r1, NO - 1, l * 16 + (NO - 1))
                spread(l * 2)
                with pe.Fori(0, NF // 4) as i:
                    for c in range(4):
                        h = hl_ + OF // 2 + i * 2
                        pe.wait_ge(lo_ready, h * 2 + (c + 3))
                        pe.wait_ge(dve_out_freed, do + DF + i * 4 + (c + 1))
                        for k in range(KD):
                            if c == 0 and k % 2 == 0:
                                pe.wait_ge(x_ready, l * 8 + (4 + k // 2 + 1))
                            m = products(c, c % 2, [(k, k)], xh, xl, k == 0, k == KD - 1)
                        m.then_inc(slab_done, 1)
                with pe.Fori(0, 4) as i:
                    pe.wait_ge(ff_ready, l * KF + KF)
                    for o in range(2):
                        for q in range(3):
                            c = 3 * o + q
                            pe.wait_ge(lo_ready, (hl_ + OG // 2 + i * 3) * 2 + (c + 3))
                            if q == 0:
                                pe.wait_ge(dve_out_freed, do + DG + i * 2 + (o + 3))
                            blocks = [(k, 8 * q + k) for k in range(min(8, KF - 8 * q))]
                            products(o, c % 2, blocks, hh, hl, q == 0, q == 2).then_inc(slab_done, 1)
                            if q == 0 and o == 1:
                                to_tokens(rst, 0, l * 16 + 8 + i * 2)
                    to_tokens(rst, 1, l * 16 + 8 + i * 2 + 1)
                spread(l * 2 + 1)

        @block.scalar
        def _(act):
            def split_hi(h, c):
                act.wait_ge(raw_loaded[c % 2], (h + (c // 2 + 1)) * 16)
                act.wait_ge(slab_done, h * 2 + (c + 1))
                act.activation(whi[:, c % 2, :], raw[:, c % 2, :], ACT.Copy).then_inc(hi_ready, 1)

            def slab_out(h, c):
                act.wait_ge(slab_done, h * 2 + (c + 3))

            def ln_part(rbuf, l, w, n):
                act.wait_ge(var_ready, n + 1)
                act.activation(lnrs[:, :], lnrs[:, :], ACT.Sqrt).then_inc(sd_ready, 1)
                for g in range(4):
                    act.wait_ge(ln_norm, n * 4 + (g + 1))
                    for m in (2 * g, 2 * g + 1):
                        gain = nrm[:, ds(l, 1), 16 * w + m]
                        shift = nrm[:, ds(l, 1), 16 * w + 8 + m]
                        act.activation(xh[:, m, :], rbuf[:, m, :], ACT.Identity, bias=shift, scale=gain)
                        x = act.activation(rbuf[:, m, :], rbuf[:, m, :], ACT.Identity, bias=shift, scale=gain)
                    x.then_inc(ln_x, 1)

            act.wait_ge(x_in, 16)
            for g in range(4):
                act.activation(xh[:, 2 * g:2 * g + 2, :], xf[:, 2 * g:2 * g + 2, :], ACT.Copy).then_inc(x_hi, 1)
            act.wait_ge(rope_arg, 1)
            act.activation(sin_t[:, :], sin_t[:, :], ACT.Sin)
            act.activation(cos_t[:, :], cos_t[:, :], ACT.Sin).then_inc(rope_done, 1)
            split_hi(0, 0)
            with act.Fori(0, L) as l:
                hl_ = l * (NSLAB // 2)
                act.wait_ge(qgate_psum, l + 1)
                act.activation(gq[:, :, :].rearrange("p t c -> p (t c)"), ps[:, 7, 0:96], ACT.Tanh, scale=0.5).then_inc(qgate_tanh, 1)

                def project(n, off, dst):
                    with act.Fori(0, n // 2) as i:
                        h = hl_ + off // 2 + i
                        for c in range(2):
                            split_hi(h, c + 1)
                            slab_out(h, c)
                            act.activation(pa[:, ds(i * 2 + (dst + c), 1), :].rearrange("p a n -> p (a n)"), ps[:, c, :], ACT.Copy)\
                               .then_inc(act_out_freed, 1)

                project(NA1, OA1, 0)
                act.wait_ge(vtok_psum, l * 2 + 2)
                act.activation(vtok[:, :, :, :].rearrange("p v t d -> p (v t d)"), ps[:, 2:4, :].rearrange("p b n -> p (b n)"), ACT.Copy)\
                   .then_inc(vtok_ready, 1)
                act.activation(st[:, 0, :], smv("ldt"), ACT.Exp).then_inc(dt_ready, 1)

                def a2_split(i):
                    split_hi(hl_ + (OA2 + i - i % 2) // 2, i % 2 + 1)

                def a2_out(i):
                    slab_out(hl_ + (OA2 + i - i % 2) // 2, i % 2)
                    act.activation(pa[:, 6 + i, :], ps[:, i % 2, :], ACT.Copy).then_inc(act_out_freed, 1)

                a2_split(0)
                a2_out(0)
                a2_split(1)
                act.wait_ge(angle_ready, l + 1)
                for t in range(9):
                    act.activation(rp[:, t, :], st[:, 1, :], ACT.Exp, scale=float(t))
                act.activation(php[:, 1, 1, :], st[:, 2, :], ACT.Sin)
                act.activation(php[:, 0, 1, :], st[:, 3, :], ACT.Sin).then_inc(sincos_ready, 1)
                a2_out(1)
                a2_split(2)
                act.wait_ge(hid_psum, l + 1)
                b1 = smv("b1")
                for i in range(4):
                    x = act.activation(hid[:, i, :], ps[:, 4, 62 * i:62 * i + 62], ACT.Identity, bias=b1[:, i:i + 1])
                x.then_inc(hid_biased, 1)
                act.wait_ge(gelu_arg, l * 5 + 1)
                act.activation(hgt[:, :, :], hgt[:, :, :], ACT.Tanh, scale=GELU_B).then_inc(gelu_tanh, 1)
                a2_out(2)
                a2_split(3)
                a2_out(3)
                act.wait_ge(kc_psum, l + 1)

                def s5_mats(b):
                    act.wait_ge(vt_psum, b + 1)
                    act.activation(vt[:, :, :, :].rearrange("p q g n -> p (q g n)"), ps[:, 4:6, :].rearrange("p b n -> p (b n)"), ACT.Copy)\
                       .then_inc(vt_ready, 1)
                    act.wait_ge(ka_psum, b + 1)
                    for par in range(2):
                        x = act.activation(kam[:, :, :].rearrange("p (g q) n -> p q g n", q=2)[:, par, :, :],
                                           ps[0:SC, 2 + par, :].rearrange("p (g n) -> p g n", g=4), ACT.Copy)
                    x.then_inc(ka_copied, 1)

                def s5_chunk(b, h, j):
                    split_hi(h, 1)
                    slab_out(h, 0)
                    act.activation(upool[:, ds(j, 1), :].rearrange("p a n -> p (a n)"), ps[:, 0, :], ACT.Copy).then_inc(act_out_freed, 1)
                    split_hi(h, 2)
                    act.wait_ge(y_psum, b + 1)
                    for par in range(2):
                        x = act.activation(y8[:, :, :].rearrange("p (g q) n -> p q g n", q=2)[:, par, :, :],
                                           ps[:, 6 + par, 0:4 * NCH].rearrange("p (g n) -> p g n", g=4), ACT.Copy)
                    x.then_inc(y8_ready, 1)
                    slab_out(h, 1)
                    act.activation(gates[:, ds(j, 1), :].rearrange("p a n -> p (a n)"), ps[:, 1, :], ACT.Tanh, scale=0.5).then_inc(act_out_freed, 1)

                s5_mats(l * 4)
                with act.Fori(0, 3) as j:
                    s5_chunk(l * 4 + j, hl_ + OB1 // 2 + j, j)
                    s5_mats(l * 4 + j + 1)
                s5_chunk(l * 4 + 3, hl_ + OB1 // 2 + 3, 3)
                with act.Fori(0, 4) as j:
                    b = l * 4 + j
                    h = hl_ + OB2 // 2 + j * 2
                    split_hi(h, 1)
                    slab_out(h, 0)
                    act.wait_ge(q_ready, b + 1)
                    act.activation(qraw[:, :], ps[:, 0, :], ACT.Copy).then_inc(act_out_freed, 1)

                    def gate(c):
                        slab_out(h, c)
                        act.activation(gates[:, ds(j * 3 + (3 + c), 1), :].rearrange("p a n -> p (a n)"), ps[:, c % 2, :], ACT.Tanh, scale=0.5)\
                           .then_inc(act_out_freed, 1)

                    split_hi(h, 2)
                    gate(1)
                    act.wait_ge(gelu_arg, l * 5 + j + 2)
                    act.activation(ygt[:, :], ygt[:, :], ACT.Tanh, scale=GELU_B).then_inc(gelu_tanh, 1)
                    act.wait_ge(ygelu_ready, b + 1)
                    act.activation(ysh[:, ds(j, 1), :].rearrange("p a (n t) -> p (a n) t", t=TAP), ygt[:, :].rearrange("p (t n) -> p n t", n=NCH), ACT.Copy, scale=0.5)\
                       .then_inc(ys_hi, 1)
                    split_hi(h, 3)
                    gate(2)
                    act.wait_ge(cs_shift, b + 1)
                    act.activation(pc[:, :, :], pc[:, :, :], ACT.Exp, scale=SCALE).then_inc(cs_exp, 1)
                    split_hi(h, 4)
                    gate(3)

                    def exps(s):
                        n = P * (s % 4 + 1)
                        act.wait_ge(s_max, b * 8 + (s + 1))
                        for br in range(2):
                            x = act.activation(prob[:, s % 2, br, 0:n], ps[:, sbank(s) + br, 0:n], ACT.Exp, scale=SCALE,
                                               bias=tiny[:, 28 + 8 * (s % 2) + br:29 + 8 * (s % 2) + br],
                                               accum_out=tiny[:, 30 + 8 * (s % 2) + br:31 + 8 * (s % 2) + br])
                        x.then_inc(s_exp, 1)

                    exps(0)
                    act.wait_ge(cs_tpsum, b + 1)
                    act.activation(pct[0:NCMP, :, :].rearrange("p s n -> p (s n)"), ps[0:NCMP, 2:4, :].rearrange("p b n -> p (b n)"), ACT.Copy)\
                       .then_inc(cs_tready, 1)
                    exps(1)
                    for s in range(8):
                        n = P * (s % 4 + 1)
                        act.wait_ge(s_tpsum, b * 8 + (s + 1))
                        act.activation(probt[:, s % 2, 0, 0:n], ps[:, 2, 0:n], ACT.Copy).then_inc(pt_sel, 1)
                        if s < 6:
                            exps(s + 2)
                    act.wait_ge(o_psum, b * 8 + 8)
                    act.activation(nsh[:, ds(j, 1), :].rearrange("p a n -> p (a n)"), ps[:, 7, :], ACT.Copy).then_inc(o_hi, 1)
                for g in range(4):
                    act.wait_ge(mix_psum, l * 4 + (g + 1))
                    act.activation(plh[:, g, :], ps[:, 4 + g, :], ACT.Copy, scale=smv("psc")[:, g:g + 1]).then_inc(mix_hi, 1)
                with act.Fori(0, NGL // 2) as i:
                    h = hl_ + OGL // 2 + i
                    for c in range(2):
                        split_hi(h, c + 1)
                        slab_out(h, c)
                        act.activation(gt[:, :], ps[:, 2 * c + 1, :], ACT.Tanh, scale=0.5).then_inc(glu_tanh, 1)
                        act.wait_ge(glu_raw, l * 4 + i * 2 + (c + 1))
                        act.activation(glh[:, ds(i * 2 + c, 1), :].rearrange("p a n -> p (a n)"), gv[:, :], ACT.Copy, scale=0.5).then_inc(glu_hi, 1)
                with act.Fori(0, 2) as i:
                    for c in range(10):
                        h = hl_ + OC // 2 + i * 5
                        split_hi(h, c + 1)
                        if c % 5 == 3:
                            slab_out(h, c)
                            act.activation(tg2[:, :, :].rearrange("p b n -> p (b n)"), ps[:, 0:2, :].rearrange("p b n -> p (b n)"), ACT.Tanh, scale=0.5)\
                               .then_inc(mg_tanh, 1)
                        if c % 5 == 4:
                            act.wait_ge(mg_raw, l * 4 + i * 2 + (c // 5 + 1))
                            act.activation(mgh[:, ds(i * 4 + 2 * (c // 5), 2), :], acc[:, :, :], ACT.Copy, scale=0.5).then_inc(mg_hi, 1)
                for c in range(NO):
                    split_hi(hl_ + OO // 2, c + 1)
                ln_part(r1, l, 0, l * 2)
                with act.Fori(0, NF // 4) as i:
                    h = hl_ + OF // 2 + i * 2
                    for c in range(4):
                        split_hi(h, c + 1)
                        if c % 2 == 0:
                            slab_out(h, c)
                            act.activation(ft[:, c // 2, :], ps[:, c, :], ACT.Tanh, scale=0.5).then_inc(ff_tanh, 1)
                        else:
                            act.wait_ge(ff_raw, l * KF + i * 2 + (c // 2 + 1))
                            act.activation(hh[:, ds(i * 2 + c // 2, 1), :].rearrange("p a n -> p (a n)"), fb[:, c // 2, :], ACT.Copy, scale=0.5)\
                               .then_inc(ff_hi, 1)
                with act.Fori(0, 4) as i:
                    h = hl_ + OG // 2 + i * 3
                    for o in range(2):
                        for q in range(3):
                            split_hi(h, 3 * o + q + 1)
                        act.wait_ge(r_ready, l * 16 + 8 + i * 2 + (o + 1))
                        act.activation(xf[:, ds(i * 2 + o, 1), :].rearrange("p a n -> p (a n)"), rst[:, o, :], ACT.Copy).then_inc(r_kept, 1)
                ln_part(xf, l, 1, l * 2 + 1)

        @block.vector
        def _(dve):
            def split_lo(h, c):
                dve.wait_ge(hi_ready, h * 2 + (c + 1))
                dve.tensor_tensor(wlo[:, c % 2, :], raw[:, c % 2, :], whi[:, c % 2, :].bitcast(f32), SUB).then_inc(lo_ready, 1)

            def slab_out(h, c):
                dve.wait_ge(slab_done, h * 2 + (c + 3))

            def tt(o, a, b, op):
                return dve.tensor_tensor(o, a, b, op)

            def cmul(orr, oi, ar, ai, br, bi, t1, t2, conj=False, neg_i=False):
                tt(t1, ar, br, MUL)
                tt(t2, ai, bi, MUL)
                dve.drain()
                tt(orr, t1, t2, ADD if conj else SUB)
                dve.drain()
                tt(t1, ar, bi, MUL)
                tt(t2, ai, br, MUL)
                dve.drain()
                if neg_i:
                    return dve.scalar_tensor_tensor(oi, t1, -1.0, t2, MUL, SUB)
                return tt(oi, t1, t2, SUB if conj else ADD)

            def to_phase(x, co, k):
                dve.tensor_scalar(k, x, 1.0 / (2 * math.pi), MAGIC, MUL, ADD)
                dve.drain()
                dve.tensor_scalar(k, k, MAGIC, None, SUB)
                dve.drain()
                for part in (TWO_PI_1, TWO_PI_2, TWO_PI_3):
                    dve.scalar_tensor_tensor(x, k, -part, x, MUL, ADD)
                    dve.drain()
                dve.tensor_scalar(x, x, PI_F, -PI_F, MIN, MAX)
                dve.drain()
                dve.scalar_tensor_tensor(co, x, -1.0, x, MUL, MAX)
                dve.drain()
                return dve.tensor_scalar(co, co, -1.0, math.pi / 2, MUL, ADD)

            def gelu(y, t, n):
                tt(t, y, y, MUL)
                dve.drain()
                dve.tensor_scalar(t, t, GELU_A, 1.0, MUL, ADD)
                dve.drain()
                tt(t, t, y, MUL).then_inc(gelu_arg, 1)
                dve.wait_ge(gelu_tanh, n + 1)
                return dve.scalar_tensor_tensor(t, t, 1.0, y, ADD, MUL)

            def residual(dst, m, bank, x_m):
                dve.scalar_tensor_tensor(dst, xh[:, x_m, :].bitcast(f32), ALPHA, ps[:, bank, :], MUL, ADD).then_inc(dve_out_freed, 1)
                dve.drain()
                return dve.scalar_tensor_tensor(dst, xl[:, x_m, :].bitcast(f32), ALPHA, dst, MUL, ADD).then_inc(r_ready, 1)

            def stats(m, bank, count):
                dve.wait_ge(rt_psum, count + 1)
                for t in range(4):
                    x = dve.bn_stats(lnst[:, t, m, :], ps[:, bank, P * t:P * t + P])
                x.then_inc(stats_done, 1)

            def ln_part(rbuf, n):
                dve.drain()
                for t in range(4):
                    dve.bn_aggr(lnmv[:, t, :], lnst[:, t, :, :].rearrange("p m s -> p (m s)"))
                dve.drain()
                dve.tensor_scalar(lnrs[:, :], lnmv[:, :, 1], EPS, None, ADD).then_inc(var_ready, 1)
                dve.tensor_copy(lnbc[:, 0, :, :], bc(lnmv[:, :, 0], 2, P))
                dve.wait_ge(sd_ready, n + 1)
                dve.reciprocal(lnrs[:, :], lnrs[:, :])
                dve.drain()
                dve.tensor_copy(lnbc[:, 1, :, :], bc(lnrs[:, :], 2, P)).then_inc(ln_bc, 1)
                dve.wait_ge(ln_psum, n + 1)
                for g in range(5):
                    if g < 4:
                        v = rbuf[:, 2 * g:2 * g + 2, :]
                        tt(v, v, bc(ps[:, 6, :], 1, 2), SUB)
                        dve.drain()
                        tt(v, v, bc(ps[:, 7, :], 1, 2), MUL).then_inc(ln_norm, 1)
                    if g:
                        dve.wait_ge(ln_x, n * 4 + g)
                        tt(xl[:, 2 * g - 2:2 * g, :], rbuf[:, 2 * g - 2:2 * g, :], xh[:, 2 * g - 2:2 * g, :].bitcast(f32), SUB).then_inc(x_ready, 1)

            dve.memset(tiny[:, 0:1], 0.0).then_inc(lo_ready, 2)
            dve.memset(tiny[:, 1:2], 0.0).then_inc(slab_done, 2)
            dve.memset(tiny[:, 2:3], 0.0).then_inc(act_out_freed, 2)
            dve.memset(tiny[:, 3:4], 0.0).then_inc(dve_out_freed, 4)
            dve.memset(tiny[:, 4:5], 0.0).then_inc(stats_done, 2)
            dve.memset(tiny[:, 5:6], 0.0).then_inc(o_ready, 1)
            dve.memset(tiny[:, 6:7], 0.0).then_inc(mix_ready, 1)
            dve.memset(tiny[:, 7:8], 0.0).then_inc(y8_ready, 1)
            dve.memset(tiny[:, 8:9], 0.0).then_inc(q_ready, 1)
            dve.wait_ge(consts_in, 48)
            dve.tensor_copy(kro[:, 1, :], kro[:, 0, :].bitcast(i32))
            dve.drain()
            dve.tensor_scalar(sin_t[:, :], kro[:, 1, :], cnv("inv"), None, MUL)
            dve.drain()
            to_phase(sin_t[:, :], cos_t[:, :], kro[:, 1, :]).then_inc(rope_arg, 1)
            for g in range(4):
                dve.wait_ge(x_hi, g + 1)
                v = slice(2 * g, 2 * g + 2)
                tt(xl[:, v, :], xf[:, v, :], xh[:, v, :].bitcast(f32), SUB).then_inc(x_ready, 1)
            split_lo(0, 0)
            dve.wait_ge(rope_done, 1)

            with dve.Fori(0, L) as l:
                hl_ = l * (NSLAB // 2)
                ao = l * ACT_OUTS
                with dve.Fori(0, NA1 // 2) as i:
                    for c in range(2):
                        split_lo(hl_ + i, c + 1)
                dve.wait_ge(qgate_tanh, l + 1)
                dve.tensor_scalar(gq[:, :, :], gq[:, :, :], 1.0, 0.5, ADD, MUL)
                for i in range(3):
                    dve.wait_ge(krot_psum, l * 3 + (i + 1))
                    tt(rt1[:, :], pa[:, i, :], cos_t[:, :], MUL)
                    tt(rt2[:, :], ps[:, 4 + i, :], sin_t[:, :], MUL)
                    dve.drain()
                    if i < 2:
                        tt(kro[:, i, :], rt1[:, :], rt2[:, :], ADD).then_inc(krot_done, 1)
                    else:
                        v = "p (m e) -> p m e"
                        tt(zpm[:, 0, :, :].rearrange("p e m -> p m e"), rt1[:, :].rearrange(v, e=2), rt2[:, :].rearrange(v, e=2), ADD)\
                            .then_inc(krot_done, 1)
                    dve.drain()
                dve.memset(tiny[:, 0:1], 0.0).then_inc(z_perm, 1)
                dve.tensor_copy(zpm[:, 1, :, :].rearrange("p e m -> p m e"), pa[:, 3, :].rearrange("p (m e) -> p m e", e=2)).then_inc(z_perm, 1)
                dve.wait_ge(dt_ready, l + 1)
                are, aim = smv("are"), smv("aim")
                tt(st[:, 1, :], are, st[:, 0, :], MUL)
                tt(st[:, 2, :], aim, st[:, 0, :], MUL)
                dve.drain()
                to_phase(st[:, 2, :], st[:, 3, :], st[:, 4, :]).then_inc(angle_ready, 1)

                def a2_lo(i):
                    split_lo(hl_ + (OA2 + i - i % 2) // 2, i % 2 + 1)

                a2_lo(0)
                a2_lo(1)
                for j in range(2):
                    dve.wait_ge(z2_in[j], (l + 1) * 64)
                    for a in range(2):
                        x = tt(zb[:, j, 8 * a:8 * a + 8, :, :], z2[:, j, :, 8 * a:8 * a + 8 * NCMP].rearrange("p h (n t) -> p t h n", t=8),
                               smv("pos")[:, 16 * j + 8 * a:16 * j + 8 * a + 8].unsqueeze(2).unsqueeze(3).to_broadcast([P, 8, 2, NCMP]), ADD)
                    x.then_inc(z_ready, 1)
                dve.memset(php[:, 0, 0, :], 1.0)
                dve.memset(php[:, 1, 0, :], 0.0)
                dve.memset(hst[:, :, :, 0:1], 0.0)
                dve.memset(eph[:, 0, :, 0:1], 1.0)
                dve.memset(eph[:, 1, :, 0:1], 0.0)
                dve.wait_ge(sincos_ready, l + 1)
                for w in (1, 2, 4):
                    lo, n = slice(1, w + 1), slice(w + 1, 2 * w + 1)
                    pr, pi = bc(php[:, 0, w, :], 1, w), bc(php[:, 1, w, :], 1, w)
                    cmul(php[:, 0, n, :], php[:, 1, n, :], php[:, 0, lo, :], php[:, 1, lo, :], pr, pi, lam[:, 0, lo, :], lam[:, 1, lo, :])
                    dve.drain()
                tt(lam[:, 0, :, :], php[:, 0, :, :], rp[:, :, :], MUL)
                tt(lam[:, 1, :, :], php[:, 1, :, :], rp[:, :, :], MUL)
                dve.drain()
                dve.tensor_scalar(st[:, 5, :], lam[:, 0, 1, :], 1.0, None, SUB)
                tt(st[:, 6, :], are, are, MUL)
                tt(st[:, 7, :], aim, aim, MUL)
                dve.drain()
                tt(st[:, 6, :], st[:, 6, :], st[:, 7, :], ADD)
                dve.drain()
                dve.reciprocal(st[:, 6, :], st[:, 6, :])
                cmul(st[:, 8, :], st[:, 9, :], are, aim, st[:, 5, :], lam[:, 1, 1, :], st[:, 10, :], st[:, 11, :], conj=True)
                dve.drain()
                tt(coef[:, 0, :], st[:, 8, :], st[:, 6, :], MUL)
                tt(coef[:, 1, :], st[:, 9, :], st[:, 6, :], MUL)
                dve.tensor_copy(eph[:, :, :, 1], php[:, :, 8, :])
                dve.drain()
                w = 1
                while 2 * w < NCH:
                    cmul(st[:, 12, :], st[:, 13, :], eph[:, 0, :, w], eph[:, 1, :, w], eph[:, 0, :, w], eph[:, 1, :, w], st[:, 14, :], st[:, 15, :])
                    dve.drain()
                    w *= 2
                    old, new = slice(0, w), slice(w, 2 * w)
                    t1 = r8m[:, :, 0:w]
                    t2 = r8m[:, :, w:2 * w]
                    cmul(eph[:, 0, :, new], eph[:, 1, :, new], eph[:, 0, :, old], eph[:, 1, :, old],
                         bc(st[:, 12, :], 2, w), bc(st[:, 13, :], 2, w), t1, t2)
                    dve.drain()
                dve.tensor_copy(r8m[:, :, :], bc(rp[:, 8, :], 2, NCH))
                dve.drain()
                dve.memset(r8m[:, :, 0:1], 0.0)
                a2_lo(2)
                dve.wait_ge(hid_biased, l + 1)
                gelu(hid[:, :, :], hgt[:, :, :], l * 5).then_inc(hid_ready, 1)

                def blocks_of(j):
                    for t in range(TAP):
                        u = pa[:, ds(j + 6, 1), :].rearrange("p a (n t) -> p (a t) n", t=TAP)[:, TAP - 1 - t, :]
                        x = dve.tensor_copy(ubl[:, t, :], u)
                    x.then_inc(ubl_ready, 1)

                def par_c(name, j):
                    return smv(name, GP, SC)[:, ds(j * 4, 4), :]

                def over(tab, q, n, j):
                    return tab[:, q, 0:n, ds(j * 4, 4)].rearrange("p t g -> p g t").unsqueeze(3).to_broadcast([P, 4, n, SC])

                def taps(x, n):
                    return x.unsqueeze(2).to_broadcast([P, 4, n, SC])

                v4 = "p (g t c) -> p g t c"

                def input_mats(j):
                    dve.drain()
                    t1, t2 = ta[:, 0:64].rearrange("p (g c) -> p g c", g=4), tb[:, 0:64].rearrange("p (g c) -> p g c", g=4)
                    cmul(bch[:, 0, :, :], bch[:, 1, :, :], bc(coef[:, 0, ds(j * 4, 4)], 2, SC), bc(coef[:, 1, ds(j * 4, 4)], 2, SC),
                         par_c("bre", j), par_c("bim", j), t1, t2)
                    dve.drain()
                    t1, t2 = ta[:, 0:512].rearrange(v4, g=4, c=SC), tb[:, 0:512].rearrange(v4, g=4, c=SC)
                    cmul(vmat[:, 0, :, :].rearrange("p g (t c) -> p g t c", c=SC), vmat[:, 1, :, :].rearrange("p g (t c) -> p g t c", c=SC),
                         over(lam, 0, 8, j), over(lam, 1, 8, j), taps(bch[:, 0, :, :], 8), taps(bch[:, 1, :, :], 8), t1, t2)

                def output_mats(j):
                    t1, t2 = ta[:, :].rearrange(v4, g=4, c=SC), tb[:, :].rearrange(v4, g=4, c=SC)
                    cmul(wmat[:, 0, :, :].rearrange("p g (t c) -> p g t c", c=SC), wmat[:, 1, :, :].rearrange("p g (t c) -> p g t c", c=SC),
                         over(lam, 0, 9, j), over(lam, 1, 9, j), taps(par_c("cre", j), 9), taps(par_c("cim", j), 9), t1, t2, neg_i=True).then_inc(mats_ready, 1)
                    tt(skip[:, :, :], bc(cnv("ident")[0:SC, 0:SC], 1, 8), bc(smv("dsk")[0:SC, ds(j * 8, 8)], 2, SC), MUL)
                    dve.drain()

                def add_skip(b):
                    dve.wait_ge(ka_copied, b + 1)
                    tt(kam[:, :, 0:SC], kam[:, :, 0:SC], skip[:, :, :], ADD).then_inc(ka_ready, 1)

                dve.wait_ge(act_out_freed, ao + 2 + (OA2 + 1))
                blocks_of(0)
                input_mats(0)
                dve.wait_ge(kc_psum, l + 1)
                dve.tensor_scalar(kct[:, :], ps[:, 5, 0:NCMP], 0.5, None, MUL)
                dve.tensor_scalar(vct[0:NCMP, :, :].rearrange("p h d -> p (h d)"), ps[0:NCMP, 6, 0:2 * HD], 0.5, None, MUL).then_inc(kc_ready, 1)
                a2_lo(3)
                dve.drain()
                output_mats(0)
                add_skip(l * 4)

                def s5_chunk(b, h, j, last):
                    split_lo(h, 1)
                    g4 = ds(j * 4, 4)
                    dve.wait_ge(x_state_psum, b + 1)
                    xs = [ps[:, 4, 4 * NCH * q:4 * NCH * (q + 1)] for q in range(2)]
                    er, ei = (eph[:, q, g4, :].rearrange("p g n -> p (g n)") for q in range(2))
                    sr, si = (srot[:, q, :, :].rearrange("p g n -> p (g n)") for q in range(2))
                    t1, t2 = ta[:, 0:256], tb[:, 0:256]
                    cmul(sr, si, er, ei, xs[0], xs[1], t1, t2, conj=True)
                    dve.drain()
                    for q in range(2):
                        dve.tensor_tensor_scan(gsc[:, q, :, :].rearrange("p g n -> p (g n)"), r8m[:, g4, :].rearrange("p g n -> p (g n)"),
                                               srot[:, q, :, :].rearrange("p g n -> p (g n)"), 0.0, MUL, ADD)
                    dve.drain()
                    v3 = "p (g n) -> p g n"
                    cmul(hst[:, 0, :, 1:NCH + 1], hst[:, 1, :, 1:NCH + 1], eph[:, 0, g4, :], eph[:, 1, g4, :], gsc[:, 0, :, :], gsc[:, 1, :, :],
                         t1.rearrange(v3, g=4), t2.rearrange(v3, g=4)).then_inc(h_ready, 1)
                    if not last:
                        dve.wait_ge(act_out_freed, ao + 2 + OB1)
                        blocks_of(j + 1)
                        input_mats(j + 1)
                    split_lo(h, 2)
                    if not last:
                        dve.drain()
                        dve.wait_ge(y_psum, b + 1)
                        output_mats(j + 1)
                        add_skip(b + 1)

                with dve.Fori(0, 3) as j:
                    s5_chunk(l * 4 + j, hl_ + OB1 // 2 + j, j, False)
                s5_chunk(l * 4 + 3, hl_ + OB1 // 2 + 3, 3, True)

                with dve.Fori(0, 4) as j:
                    b = l * 4 + j
                    h = hl_ + OB2 // 2 + j * 2
                    split_lo(h, 1)
                    split_lo(h, 2)
                    dve.wait_ge(q_rot_psum, b + 1)
                    tt(qt1[:, :], qraw[:, :], cos_t[:, :], MUL)
                    tt(qt2[:, :], ps[:, 6, :], sin_t[:, :], MUL)
                    dve.drain()
                    tt(qro[:, :], qt1[:, :], qt2[:, :], ADD).then_inc(q_ready, 1)
                    dve.wait_ge(yfm_in, (l + 1) * 64)
                    gelu(yfm[:, ds(j, 1), :].rearrange("p a n -> p (a n)"), ygt[:, :], l * 5 + j + 1).then_inc(ygelu_ready, 1)
                    split_lo(h, 3)
                    dve.wait_ge(ys_hi, b + 1)
                    o = ysl[:, ds(j, 1), :].rearrange("p a (n t) -> p (a n) t", t=TAP)
                    dve.scalar_tensor_tensor(o, ygt[:, :].rearrange("p (t n) -> p n t", n=NCH), 0.5,
                                             ysh[:, ds(j, 1), :].rearrange("p a (n t) -> p (a n) t", t=TAP).bitcast(f32), MUL, SUB).then_inc(ys_ready, 1)
                    dve.wait_ge(cs_psum, b + 1)
                    c2 = pc[:, :, :].rearrange("p (v t) n -> p v (t n)", v=2)
                    mc, sc, al = tiny[:, 0:8], tiny[:, 8:16], tiny[:, 16:24]
                    tt(c2, ps[:, 4:6, 0:4 * NCMP], bc(cnv("cadd"), 1, 2), ADD)
                    dve.drain()
                    dve.tensor_reduce(mc, pc[:, :, :], AX.X, MAX)
                    dve.drain()
                    tt(pc[:, :, :], pc[:, :, :], bc(mc, 2, NCMP), SUB).then_inc(cs_shift, 1)

                    def max_part(s):
                        t = s % 4
                        dve.wait_ge(s_psum, b * 8 + (s + 1))
                        v = ps[:, sbank(s):sbank(s) + 2, P * t:P * t + P]
                        tt(v, v, bc(cnv("dmask"), 1, 2), ADD)
                        dve.drain()
                        dve.tensor_reduce(tiny[:, 24:26], ps[:, sbank(s):sbank(s) + 2, 0:P * (t + 1)], AX.X, MAX)
                        dve.drain()
                        dve.tensor_scalar(tiny[:, 28 + 8 * (s % 2):30 + 8 * (s % 2)], tiny[:, 24:26], -SCALE, None, MUL).then_inc(s_max, 1)

                    split_lo(h, 4)
                    dve.wait_ge(cs_exp, b + 1)
                    dve.tensor_reduce(sc, pc[:, :, :], AX.X, ADD)
                    dve.drain()
                    dve.reciprocal(sc, sc)
                    dve.drain()
                    for kv in range(2):
                        tt(al[:, 4 * kv:4 * kv + 4], sc[:, 4 * kv:4 * kv + 4], gq[:, :, ds(j * 6 + 3 * kv, 1)].rearrange("p t a -> p (t a)"), MUL)
                    dve.drain()
                    tt(pc[:, :, :], pc[:, :, :], bc(al, 2, NCMP), MUL)
                    dve.drain()
                    tt(c2, c2, bc(cnv("c01"), 1, 2), MUL).then_inc(cs_ready, 1)

                    def scale(s):
                        kv, t = s // 4, s % 4
                        n = P * (t + 1)
                        sums, rat = tiny[:, 30 + 8 * (s % 2):32 + 8 * (s % 2)], tiny[:, 44 + 2 * (s % 2):46 + 2 * (s % 2)]
                        dve.wait_ge(s_exp, b * 8 + (s + 1))
                        dve.reciprocal(rat, sums)
                        dve.drain()
                        tt(rat, rat, gq[:, t, ds(j * 6 + (3 * kv + 1), 2)], MUL)
                        dve.drain()
                        for br in range(2):
                            x = dve.tensor_scalar(prob[:, s % 2, br, 0:n], prob[:, s % 2, br, 0:n], rat[:, br:br + 1], None, MUL)
                        x.then_inc(s_ready, 1)

                    max_part(0)
                    dve.drain()
                    scale(0)
                    max_part(1)
                    for s in range(8):
                        n = P * (s % 4 + 1)
                        dve.wait_ge(s_tpsum, b * 8 + (s + 1))
                        dve.tensor_copy(probt[:, s % 2, 1, 0:n], ps[:, 3, 0:n]).then_inc(pt_win, 1)
                        if s < 7:
                            scale(s + 1)
                        if s < 6:
                            max_part(s + 2)
                    dve.wait_ge(o_hi, b + 1)
                    tt(nsl[:, ds(j, 1), :].rearrange("p a n -> p (a n)"), ps[:, 7, :],
                       nsh[:, ds(j, 1), :].rearrange("p a n -> p (a n)").bitcast(f32), SUB).then_inc(o_ready, 1)

                src = upool
                for k in range(4):
                    w, dst = 1 << k, (pla, plb)[k % 2]
                    tt(dst[:, k:4, w:S], src[:, k:4, w:S], src[:, k:4, 0:S - w], ADD)
                    dve.tensor_copy(dst[:, k:4, 0:w], src[:, k:4, 0:w])
                    dve.drain()
                    src = dst
                for g in range(4):
                    w = 2 << g
                    v = (pla, plb)[g % 2][:, g, :]
                    ic = cnv("icnt")[:, 16 * g:16 * g + w]
                    tt(v[:, 0:w], v[:, 0:w], ic, MUL)
                    dve.scalar_tensor_tensor(v[:, w:S], v[:, w:S], 1.0 / w, upool[:, g, w:S], MUL, SUB)
                    dve.drain()
                    x = tt(v[:, 0:w], v[:, 0:w], upool[:, g, 0:w], SUB)
                x.then_inc(pool_ready, 1)
                for g in range(4):
                    dve.wait_ge(mix_hi, l * 4 + (g + 1))
                    dve.scalar_tensor_tensor(pll[:, g, :], ps[:, 4 + g, :], smv("psc")[:, g:g + 1], plh[:, g, :].bitcast(f32), MUL, SUB)\
                       .then_inc(mix_ready, 1)
                with dve.Fori(0, NGL // 2) as i:
                    h = hl_ + OGL // 2 + i
                    for c in range(2):
                        split_lo(h, c + 1)
                        dve.wait_ge(glu_tanh, l * 4 + i * 2 + (c + 1))
                        dve.scalar_tensor_tensor(gv[:, :], gt[:, :], 1.0, ps[:, 2 * c, :], ADD, MUL).then_inc(glu_raw, 1)
                        dve.wait_ge(glu_hi, l * 4 + i * 2 + (c + 1))
                        o = ds(i * 2 + c, 1)
                        dve.scalar_tensor_tensor(gll[:, o, :].rearrange("p a n -> p (a n)"), gv[:, :], 0.5,
                                                 glh[:, o, :].rearrange("p a n -> p (a n)").bitcast(f32), MUL, SUB).then_inc(glu_ready, 1)
                        dve.drain()
                        dve.memset(tiny[:, 0:1], 0.0).then_inc(dve_out_freed, 2)
                with dve.Fori(0, 2) as i:
                    h = hl_ + OC // 2 + i * 5
                    for c in range(10):
                        split_lo(h, c + 1)
                        q, pr = c % 5, c // 5
                        flat = "p b n -> p (b n)"
                        if q in (0, 1):
                            dst = (acc, tmp)[q]
                            dve.drain()
                            slab_out(h, c)
                            dve.scalar_tensor_tensor(dst[:, :, :].rearrange(flat), gates[:, ds(i * 4 + (2 * pr + 8 * q), 2), :].rearrange(flat), 1.0,
                                                     ps[:, 2 * q:2 * q + 2, :].rearrange(flat), ADD, MUL).then_inc(dve_out_freed, 2)
                        if q == 4:
                            slab_out(h, c)
                            dve.wait_ge(mg_tanh, l * 4 + i * 2 + (pr + 1))
                            dve.scalar_tensor_tensor(tmp[:, :, :].rearrange(flat), tg2[:, :, :].rearrange(flat), 1.0,
                                                     ps[:, 2:4, :].rearrange(flat), ADD, MUL).then_inc(dve_out_freed, 4)
                        if q in (1, 4):
                            dve.drain()
                            x = tt(acc[:, :, :], acc[:, :, :], tmp[:, :, :], ADD)
                            dve.drain()
                        if q == 4:
                            x.then_inc(mg_raw, 1)
                            dve.wait_ge(mg_hi, l * 4 + i * 2 + (pr + 1))
                            o = ds(i * 4 + 2 * pr, 2)
                            dve.scalar_tensor_tensor(mgl[:, o, :], acc[:, :, :], 0.5, mgh[:, o, :].bitcast(f32), MUL, SUB).then_inc(mg_ready, 1)
                for c in range(NO):
                    split_lo(hl_ + OO // 2, c + 1)
                    slab_out(hl_ + OO // 2, c)
                    residual(r1[:, c, :], c, c % 4, c)
                    if c:
                        stats(c - 1, 4 + (c - 1) % 2, l * 16 + (c - 1))
                stats(NO - 1, 5, l * 16 + (NO - 1))
                ln_part(r1, l * 2)
                with dve.Fori(0, NF // 4) as i:
                    h = hl_ + OF // 2 + i * 2
                    for c in range(4):
                        split_lo(h, c + 1)
                        p = c // 2
                        if c % 2 == 0:
                            dve.wait_ge(ff_tanh, l * KF + i * 2 + (p + 1))
                            dve.scalar_tensor_tensor(fa[:, p, :], ft[:, p, :], 1.0, ps[:, c, :], ADD, MUL)
                        else:
                            dve.drain()
                            slab_out(h, c)
                            tt(fb[:, p, :], fa[:, p, :], ps[:, c, :], MUL).then_inc(ff_raw, 1)
                            dve.wait_ge(ff_hi, l * KF + i * 2 + (p + 1))
                            o = ds(i * 2 + p, 1)
                            dve.scalar_tensor_tensor(hl[:, o, :].rearrange("p a n -> p (a n)"), fb[:, p, :], 0.5,
                                                     hh[:, o, :].rearrange("p a n -> p (a n)").bitcast(f32), MUL, SUB).then_inc(ff_ready, 1)
                            dve.drain()
                            dve.memset(tiny[:, 0:1], 0.0).then_inc(dve_out_freed, 2)
                with dve.Fori(0, 4) as i:
                    h = hl_ + OG // 2 + i * 3
                    for o in range(2):
                        for q in range(3):
                            split_lo(h, 3 * o + q + 1)
                        slab_out(h, 3 * o + 2)
                        m1 = ds(i * 2 + o, 1)
                        flat = "p a n -> p (a n)"
                        dve.scalar_tensor_tensor(rst[:, o, :], xh[:, m1, :].rearrange(flat).bitcast(f32), ALPHA, ps[:, o, :], MUL, ADD).then_inc(dve_out_freed, 1)
                        dve.drain()
                        dve.scalar_tensor_tensor(rst[:, o, :], xl[:, m1, :].rearrange(flat).bitcast(f32), ALPHA, rst[:, o, :], MUL, ADD).then_inc(r_ready, 1)
                    for o in range(2):
                        n = l * 16 + 8 + i * 2 + o
                        dve.wait_ge(rt_psum, n + 1)
                        for t in range(4):
                            x = dve.bn_stats(lnst[:, t, ds(i * 2 + o, 1), :].rearrange("p a s -> p (a s)"), ps[:, 4 + o, P * t:P * t + P])
                        x.then_inc(stats_done, 1)
                        dve.wait_ge(r_kept, l * 8 + i * 2 + (o + 1))
                ln_part(xf, l * 2 + 1)


def packed(v):
    f = np.float32
    w_in, w_br = v["w_in"], v["w_branch"]
    heads = np.concatenate([np.r_[h * HD:(h + 1) * HD] for j in range(4) for h in (j, j + 4)])
    stream = np.zeros((L, NSLAB, P, 8, P), f)

    def chunks(w, cols):
        return w[:, cols].reshape(-1, P, len(cols)).transpose(1, 0, 2)

    for l in range(L):
        n = 0

        def put(*parts):
            nonlocal n
            at = 0
            for part in parts:
                stream[l, n, :, at:at + part.shape[1], :] = part
                at += part.shape[1]
            n += 1

        def cols(a):
            return np.arange(a, a + P)

        for a in (1792, 2048, 1536, 1664, 1920, 2176):
            put(chunks(w_in[l], cols(a)))
        for j in range(4):
            put(chunks(w_in[l], cols(P * j)))
        gate0 = 2328
        for j in range(4):
            put(chunks(w_in[l], cols(512 + P * j)))
            put(chunks(w_in[l], cols(gate0 + P * j)))
        for j in range(4):
            put(chunks(w_in[l], 1024 + heads[P * j:P * j + P]))
            for c in range(3):
                put(chunks(w_in[l], cols(gate0 + P * (4 + 3 * j + c))))
        for m in range(4):
            put(chunks(v["ssm_w_glu"][l], cols(P * m)), chunks(v["ssm_w_glu"][l], cols(512 + P * m)))
        br = [w_br[l, 0], w_br[l, 1], w_br[l, 2][heads]]
        for m in range(0, 8, 2):
            for b in (0, 1):
                put(chunks(br[b], cols(P * m)), chunks(br[b], cols(P * (m + 1))))
            for c in (0, 1):
                put(chunks(w_in[l], cols(gate0 + P * (16 + m + c))))
            put(chunks(br[2], cols(P * m)), chunks(br[2], cols(P * (m + 1))))
        for m in range(8):
            put(chunks(v["w_out"][l], cols(P * m)))
        for i in range(KF):
            put(chunks(v["ffn_w_in"][l], cols(P * i)))
            put(chunks(v["ffn_w_in"][l], cols(FF + P * i)))
        for m in range(8):
            w = chunks(v["ffn_w_out"][l], cols(P * m))
            for q in range(3):
                put(w[:, 8 * q:8 * q + 8])
        assert n == NSLAB
    w1s = v["cmp_w1"].reshape(L * 2, 16, P, CH).transpose(0, 2, 1, 3).reshape(L * 2, P, 16 * CH)
    sm = np.zeros((L, P, NSM), f)

    def fill(name, x):
        a, b = SM[name]
        sm[:, :, a:b] = x.reshape(L, P, b - a)

    def by_state(x):
        return np.moveaxis(x.reshape(L, GP, 2 * SN, *x.shape[3:]), 1, 2)

    fill("are", by_state(v["ssm_a_re"]))
    fill("aim", by_state(v["ssm_a_im"]))
    fill("ldt", by_state(np.broadcast_to(v["ssm_log_dt"][:, :, None], (L, SG, SN))))
    fill("bre", by_state(v["ssm_b_re"]))
    fill("bim", by_state(v["ssm_b_im"]))
    fill("cre", by_state(v["ssm_c_re"].transpose(0, 1, 3, 2)))
    fill("cim", by_state(v["ssm_c_im"].transpose(0, 1, 3, 2)))
    dsk = np.zeros((L, P, SG), f)
    dsk[:, 0:SC, :] = v["ssm_d"].reshape(L, SG, SC).transpose(0, 2, 1)
    fill("dsk", dsk)
    fill("psc", v["pool_scale"].reshape(L, 4, P).transpose(0, 2, 1))
    fill("b1", v["cmp_b1"].reshape(L, 4, P).transpose(0, 2, 1))
    g24 = [2304 + b * 8 + kv * 4 + j for j in range(4) for kv in range(2) for b in range(3)]
    fill("wg", v["w_in"][:, :, g24].reshape(L, KD, P, 24).transpose(0, 2, 1, 3))
    fill("wpool", v["pool_w"].transpose(0, 2, 1, 3))
    fill("w2", v["cmp_w2"].reshape(L, 4, P, HD).transpose(0, 2, 1, 3))
    fill("pos", v["cmp_pos"].reshape(L, 2, 16, P).transpose(0, 3, 1, 2))
    norms = np.zeros((P, L, 32), f)
    for w in range(2):
        norms[:, :, 16 * w:16 * w + 8] = v["ln_g"][:, w].reshape(L, KD, P).transpose(2, 0, 1)
        norms[:, :, 16 * w + 8:16 * w + 16] = v["ln_b"][:, w].reshape(L, KD, P).transpose(2, 0, 1)
    cn = np.zeros((P, NCN), f)
    i = np.arange(P)

    def const(name, x):
        a, b = CN[name]
        cn[:, a:b] = x.reshape(P, b - a)

    const("ident", np.eye(P, dtype=f))
    rot = np.zeros((P, P), f)
    for m in range(P):
        if m % HD < HD // 2:
            rot[m + HD // 2, m] = -1.0
        else:
            rot[m - HD // 2, m] = 1.0
    const("rot", rot)
    const("dmask", np.where(i[None, :] > i[:, None], NEG, 0.0).astype(f))
    tok = np.arange(4)[None, :, None] * P + i[:, None, None]
    seen = CSTR * np.arange(NCMP)[None, None, :] + 31 <= tok
    const("cadd", np.where(seen, 0.0, NEG).astype(f))
    const("c01", seen.astype(f))
    icnt = np.zeros((4, 16), f)
    for g in range(4):
        icnt[g] = 1.0 / np.minimum(np.arange(16) + 1, 2 << g)
    const("icnt", np.broadcast_to(icnt.reshape(1, 64), (P, 64)))
    inv = np.power(f(10000.0), -np.arange(0, HD, 2, dtype=f) / f(HD)).astype(f)
    const("inv", np.tile(inv, 4))
    xin = v["x"][0].T.reshape(KD, P, S).transpose(1, 0, 2)
    return {"wstream": stream.reshape(L * NSLAB, P, 1024), "w1s": w1s, "smalls": sm, "norms": norms, "consts": cn,
            "xin": xin, "pos": v["positions"].astype(np.int32)}


def kernel(**inputs):
    import concourse.bacc as bacc
    from concourse.bass_utils import run_bass_kernel_spmd

    arrays = {k: np.ascontiguousarray(a) for k, a in packed({k: np.asarray(a) for k, a in inputs.items()}).items()}
    nc = bacc.Bacc("TRN2", target_bir_lowering=False, num_devices=1)
    args = {k: nc.dram_tensor(k, a.shape, mybir.dt.from_np(a.dtype), kind="ExternalInput").ap() for k, a in arrays.items()}
    out = nc.dram_tensor("out", (P, KD, S), mybir.dt.float32, kind="ExternalOutput").ap()
    build_program(nc, out=out, **args)
    r = run_bass_kernel_spmd(nc, [arrays], core_ids=[0])
    y = r.results[0]["out"]
    return np.ascontiguousarray(y.transpose(1, 0, 2).reshape(D, S).T)[None]
```

```python
import math
from contextlib import ExitStack

import numpy as np

import concourse.bass as bass
from concourse import mybir

D, S, L, P = 1024, 512, 2, 128
KD = D // P
FF = 2816
KF = FF // P
HD, CH, NCMP, CSTR = 64, 256, 31, 16
SG, SC, SN = 32, 16, 64
TAP, NCH = 8, S // 8
GP = SG // 2
ALPHA = (2 * L) ** 0.25
EPS = 1e-5
NEG = -1e30
SCALE = HD ** -0.5
GELU_A, GELU_B = 0.044715, math.sqrt(2.0 / math.pi)
MAGIC = 12582912.0
TWO_PI_1 = 6.28125
TWO_PI_2 = 0.00193500518798828125
TWO_PI_3 = 2 * math.pi - TWO_PI_1 - TWO_PI_2
PI_F = 3.1415925

NA1, NA2, NB1, NB2, NGL, NC, NO, NF, NG = 6, 4, 2, 4, 4, 10, 8, 44, 24
OA1 = 0
OA2 = OA1 + NA1
OB1 = OA2 + NA2
OB2 = OB1 + 4 * NB1
OGL = OB2 + 4 * NB2
OC = OGL + NGL
OO = OC + 2 * NC
OF = OO + NO
OG = OF + NF
NSLAB = OG + NG
ACT_OUTS = OGL
DGL, DC, DO, DF = 0, 8, 40, 48
DG = DF + 44
DVE_OUTS = DG + 8

SM = {}
_at = 0
for _n, _w in (("are", GP), ("aim", GP), ("ldt", GP), ("bre", GP * SC), ("bim", GP * SC), ("cre", GP * SC),
               ("cim", GP * SC), ("dsk", SG), ("psc", 4), ("b1", 4), ("wg", KD * 24), ("wpool", 4 * P),
               ("w2", 4 * HD), ("pos", 2 * SC)):
    SM[_n] = (_at, _at + _w)
    _at += _w
NSM = _at
CN = {}
_at = 0
for _n, _w in (("ident", P), ("rot", P), ("dmask", P), ("cadd", 4 * NCMP), ("c01", 4 * NCMP), ("icnt", 64), ("inv", 1)):
    CN[_n] = (_at, _at + _w)
    _at += _w
NCN = _at


def build_program(nc, wstream, w1s, smalls, norms, consts, xin, pos, out):
    f32, f32r, i32 = mybir.dt.float32, mybir.dt.float32r, mybir.dt.int32
    ACT = mybir.ActivationFunctionType
    ALU = mybir.AluOpType
    AX = mybir.AxisListType
    ds = bass.ds
    ADD, SUB, MUL, MAX, MIN = ALU.add, ALU.subtract, ALU.mult, ALU.max, ALU.min

    scr_u = nc.dram_tensor("scratch_u", (SC, 8, TAP, NCH), f32).ap()
    scr_y = nc.dram_tensor("scratch_y", (SC, TAP, 8, NCH), f32).ap()
    scr_k = nc.dram_tensor("scratch_k", (SC, 8, 2 * P), f32).ap()

    base = -(-nc.sbuf_base // 32) * 32
    used = {}

    def place(name, at, shape, dt=f32):
        n = 1
        for d in shape[1:]:
            n *= d
        used[name] = (at, at + n)
        return nc.alloc_sbuf_tensor_at(name, shape, dt, offset=base + 4 * at)

    top = [0]

    def own(name, shape, dt=f32):
        n = 1
        for d in shape[1:]:
            n *= d
        n = -(-n // 8) * 8
        t = place(name, top[0], shape, dt)
        top[0] += n
        return t

    xf_at = top[0]
    xf = own("xf", [P, KD, S])
    xh = own("xh", [P, KD, S], f32r)
    xl = own("xl", [P, KD, S], f32r)
    raw = own("raw", [P, 2, 1024])
    whi = own("whi", [P, 2, 1024], f32r)
    wlo = own("wlo", [P, 2, 1024], f32r)
    big_at = top[0]
    top[0] += 2 * KF * S
    hh = place("hh", big_at, [P, KF, S], f32r)
    hl = place("hl", big_at + KF * S, [P, KF, S], f32r)
    gates = place("gates", big_at, [P, 16, S])
    r1 = place("r1", big_at, [P, KD, S])
    w1 = place("w1", big_at, [P, 2, 16 * CH])
    nsh = place("nsh", big_at + 8192, [P, 4, S], f32r)
    nsl = place("nsl", big_at + 10240, [P, 4, S], f32r)
    plh = place("plh", big_at + 12288, [P, 4, S], f32r)
    pll = place("pll", big_at + 14336, [P, 4, S], f32r)
    glh = place("glh", big_at + 16384, [P, 4, S], f32r)
    gll = place("gll", big_at + 18432, [P, 4, S], f32r)
    upool = place("upool", big_at + 20480, [P, 4, S])
    ys_at = top[0]
    ysh = own("ysh", [P, 4, S], f32r)
    ysl = own("ysl", [P, 4, S], f32r)
    mgh = place("mgh", ys_at, [P, KD, S], f32r)
    mgl = place("mgl", xf_at, [P, KD, S], f32r)
    cos_t = own("cos_t", [P, S])
    sin_t = own("sin_t", [P, S])
    kv_at = top[0]
    kro = own("kro", [P, 2, S])
    vtok = own("vtok", [P, 2, 4, P])
    toep = own("toep", [P, 8, P])
    sm = own("sm", [P, NSM])
    nrm = own("nrm", [P, L, 32])
    cn = own("cn", [P, NCN])
    kct = own("kct", [P, NCMP])
    vct = own("vct", [32, 2, HD])
    gq = own("gq", [P, 4, 24])
    tiny = own("tiny", [P, 64])
    carry = own("carry", [1, 8])
    pa = place("pa", big_at + 8192, [P, 10, S])
    at = big_at + 8192 + 10 * S

    def more(name, shape):
        nonlocal at
        t = place(name, at, shape)
        at += -(-int(np.prod(shape[1:])) // 8) * 8
        return t

    eph = more("eph", [P, 2, GP, NCH])
    r8m = more("r8m", [P, GP, NCH])
    lam = more("lam", [P, 2, 9, GP])
    php = more("php", [P, 2, 9, GP])
    coef = more("coef", [P, 2, GP])
    rp = more("rp", [P, 9, GP])
    st = more("st", [P, 16, GP])
    ubl = more("ubl", [P, TAP, NCH])
    hst = more("hst", [P, 2, 4, NCH + 1])
    bch = more("bch", [P, 2, 4, SC])
    ta = more("ta", [P, 576])
    tb = more("tb", [P, 576])
    gqt = more("gqt", [24, S])
    assert at <= big_at + 20480, at - big_at
    at = big_at + 4096
    srot = more("srot", [P, 2, 4, NCH])
    gsc = more("gsc", [P, 2, 4, NCH])
    y8 = more("y8", [P, 8, NCH])
    assert at <= big_at + 6144
    yfm = place("yfm", big_at + 6144, [P, 4, S])
    at = xf_at
    vmat = more("vmat", [P, 2, 4, TAP * SC])
    vt = more("vt", [P, 2, 4, P])
    wmat = more("wmat", [P, 2, 4, 9 * SC])
    u8 = more("u8", [P, 8, NCH])
    assert at <= xf_at + 4096
    ygt = place("ygt", used["toep"][0], [P, S])
    kam = place("kam", ys_at, [SC, 8, P])
    skip = place("skip", ys_at + 1024, [SC, 8, SC])
    at = ys_at
    zpm = more("zpm", [P, 2, 2, S // 2])
    z2 = more("z2", [P, 2, 2, S // 2])
    zb = more("zb", [P, 2, 16, 2, NCMP])
    assert at <= ys_at + 4096
    hid = place("hid", big_at + 20480, [P, 4, 2 * NCMP])
    hgt = place("hgt", big_at + 20480 + 256, [P, 4, 2 * NCMP])
    hidt = place("hidt", big_at + 20480 + 1536, [2 * NCMP, S])
    rt1 = place("rt1", big_at + 20480 + 512, [P, S])
    rt2 = place("rt2", big_at + 20480 + 1024, [P, S])
    at = big_at + 12288
    prob = more("prob", [P, 3, 2, S])
    probt = more("probt", [P, 2, 2, S])
    pct = more("pct", [32, 8, P])
    pc = more("pc", [P, 8, NCMP])
    qraw = more("qraw", [P, S])
    qro = more("qro", [P, S])
    qt1 = place("qt1", used["toep"][0] + S, [P, S])
    qt2 = more("qt2", [P, S])
    assert at <= big_at + 20480
    pla = place("pla", xf_at, [P, 4, S])
    plb = place("plb", xf_at + 2048, [P, 4, S])
    gt = place("gt", kv_at, [P, S])
    gv = place("gv", kv_at + 512, [P, S])
    acc = place("acc", kv_at, [P, 2, S])
    tmp = place("tmp", kv_at + 1024, [P, 2, S])
    tg2 = place("tg2", big_at + 20480, [P, 2, S])
    lnbc = place("lnbc", kv_at, [P, 2, 4, P])
    lnst = place("lnst", kv_at + 1024, [P, 4, KD, 6])
    lnmv = place("lnmv", kv_at + 1024 + 192, [P, 4, 2])
    lnrs = place("lnrs", kv_at + 1024 + 200, [P, 4])
    rst = place("rst", ys_at, [P, 2, S])
    ft = place("ft", ys_at, [P, 2, S])
    fa = place("fa", ys_at + 1024, [P, 2, S])
    fb = place("fb", ys_at + 2048, [P, 2, S])

    ctx = ExitStack()
    with ctx:
        ps = ctx.enter_context(nc.psum_tensor("ps", [P, 8, S], f32))

        def sem(name):
            return ctx.enter_context(nc.semaphore(name))

        raw_loaded = [sem("raw_loaded_even"), sem("raw_loaded_odd")]
        hi_ready, lo_ready, slab_done = sem("hi_ready"), sem("lo_ready"), sem("slab_done")
        act_out_freed, dve_out_freed = sem("act_out_freed"), sem("dve_out_freed")
        x_in = [sem("x_in_%d" % g) for g in range(4)]
        x_hi, x_ready = sem("x_hi"), sem("x_ready")
        consts_in, small_in = sem("consts_in"), sem("small_in")
        w1_in = [sem("w1_keys_in"), sem("w1_values_in")]
        rope_arg, rope_done = sem("rope_arg"), sem("rope_done")
        toep_zero = sem("toep_zero")
        qgate_psum, qgate_tanh, qgate_tok, qgate_taken = (sem(n) for n in ("qgate_psum", "qgate_tanh", "qgate_tok", "qgate_taken"))
        krot_psum, krot_done = sem("krot_psum"), sem("krot_done")
        vtok_psum, vtok_ready = sem("vtok_psum"), sem("vtok_ready")
        z_perm, z_ready = sem("z_perm"), sem("z_ready")
        z2_in = [sem("z2_keys_in"), sem("z2_values_in")]
        hid_tok, hid_copied, hid_psum, hid_biased, hid_ready = (
            sem(n) for n in ("hid_tok", "hid_copied", "hid_psum", "hid_biased", "hid_ready"))
        kc_psum, kc_ready = sem("kc_psum"), sem("kc_ready")
        gelu_arg, gelu_tanh = sem("gelu_arg"), sem("gelu_tanh")
        dt_ready, angle_ready, sincos_ready = (sem(n) for n in ("dt_ready", "angle_ready", "sincos_ready"))
        ubl_ready, u_stored, u8_in = sem("ubl_ready"), sem("u_stored"), sem("u8_in")
        mats_ready, vt_psum, vt_ready, ka_psum, ka_copied, ka_ready, k_stored, toep_in = (
            sem(n) for n in ("mats_ready", "vt_psum", "vt_ready", "ka_psum", "ka_copied", "ka_ready", "k_stored", "toep_in"))
        x_state_psum, h_ready, y_psum, y8_ready, y_stored, yfm_in = (sem(n) for n in ("x_state_psum", "h_ready", "y_psum", "y8_ready", "y_stored", "yfm_in"))
        ygelu_ready, ys_hi, ys_ready = sem("ygelu_ready"), sem("ys_hi"), sem("ys_ready")
        q_rot_psum, q_ready = sem("q_rot_psum"), sem("q_ready")
        cs_psum, cs_shift, cs_exp, cs_ready, cs_tpsum, cs_tready = (sem(n) for n in ("cs_psum", "cs_shift", "cs_exp", "cs_ready", "cs_tpsum", "cs_tready"))
        s_psum, s_max, s_exp, s_ratio, p_sel, p_win, s_tpsum, pt_sel, pt_win, o_psum, o_hi, o_ready = (
            sem(n) for n in ("s_psum", "s_max", "s_exp", "s_ratio", "p_sel", "p_win", "s_tpsum", "pt_sel", "pt_win", "o_psum", "o_hi", "o_ready"))
        pool_ready, mix_psum, mix_hi, mix_ready = sem("pool_ready"), sem("mix_psum"), sem("mix_hi"), sem("mix_ready")
        glu_tanh, glu_raw, glu_hi, glu_ready = sem("glu_tanh"), sem("glu_raw"), sem("glu_hi"), sem("glu_ready")
        mg_tanh, mg_raw, mg_hi, mg_ready = sem("mg_tanh"), sem("mg_raw"), sem("mg_hi"), sem("mg_ready")
        r_ready, rt_psum, stats_done, var_ready, sd_ready, ln_bc, ln_psum, ln_norm, ln_x = (
            sem(n) for n in ("r_ready", "rt_psum", "stats_done", "var_ready", "sd_ready", "ln_bc", "ln_psum", "ln_norm", "ln_x"))
        ff_tanh, ff_raw, ff_hi, ff_ready = sem("ff_tanh"), sem("ff_raw"), sem("ff_hi"), sem("ff_ready")
        r_kept, out_done = sem("r_kept"), sem("out_done")
        block = ctx.enter_context(nc.Block())

        def sbank(s):
            return 4 if s % 2 == 0 else 0

        def smv(name, *shape):
            a, b = SM[name]
            v = sm[:, a:b]
            if len(shape) == 2:
                v = v.rearrange("p (a b) -> p a b", a=shape[0])
            return v

        def cnv(name):
            a, b = CN[name]
            return cn[:, a:b]

        def bc(ap, axis, n):
            v = ap.unsqueeze(axis)
            shape = list(v.shape)
            shape[axis] = n
            return v.to_broadcast(shape)

        @block.sync
        def _(sp):
            with sp.Fori(0, L * NSLAB // 2) as h:
                for s in range(2):
                    sp.wait_ge(lo_ready, h * 2 + (s + 1))
                    sp.dma_start(raw[:, s, :], wstream[ds(h * 2 + s, 1), :, :].rearrange("a p n -> p (a n)"))\
                        .then_inc(raw_loaded[s], 16)
            sp.wait_ge(lo_ready, L * NSLAB + 1)
            sp.dma_start(raw[:, 0, :], wstream[L * NSLAB - 1, :, :]).then_inc(raw_loaded[0], 16)
            for g in range(4):
                sp.wait_ge(ln_x, (2 * L - 1) * 4 + (g + 1))
                sp.dma_start(out[:, 2 * g:2 * g + 2, :], xf[:, 2 * g:2 * g + 2, :]).then_inc(out_done, 16)
            sp.wait_ge(out_done, 64)

        @block.gpsimd
        def _(pool):
            def wait(signal, value):
                pool.drain()
                pool.wait_ge(signal, value)
                pool.tensor_tensor(carry[:, 0:1], carry[:, 1:2], carry[:, 1:2], ADD)

            pool.dma_start(cn[:, :], consts).then_inc(consts_in, 16)
            pool.dma_start(nrm[:, :, :], norms).then_inc(consts_in, 16)
            pool.dma_start(kro[:, 0, :].bitcast(i32), pos.partition_broadcast(P)).then_inc(consts_in, 16)
            pool.memset(toep[:, :, :], 0.0).then_inc(toep_zero, 1)
            pool.memset(carry[:, :], 0.0).then_inc(toep_zero, 1)
            pool.wait_ge(toep_zero, 2)
            pool.dma_start(scr_k[:, :, 0:P], toep[0:SC, :, :]).then_inc(k_stored, 16)
            with pool.Fori(0, L) as l:
                wait(mix_ready, l * 4 + 1)
                pool.dma_start(sm[:, :], smalls[ds(l, 1), :, :].rearrange("a p n -> p (a n)")).then_inc(small_in, 16)
                wait(dve_out_freed, l * DVE_OUTS + 4)
                for j in range(2):
                    pool.dma_start(w1[:, j, :], w1s[ds(l * 2 + j, 1), :, :].rearrange("a p n -> p (a n)")).then_inc(w1_in[j], 16)
                for n, j in enumerate((1, 0)):
                    wait(z_perm, l * 2 + (n + 1))
                    for e in range(2):
                        for h in range(2):
                            pool.dma_start(z2[64 * e:64 * e + 64, j, h, :], zpm[64 * h:64 * h + 64, j, e, :]).then_inc(z2_in[j], 16)

                def store_u(b):
                    wait(ubl_ready, b + 1)
                    pool.dma_start(scr_u.rearrange("c g t n -> g c (t n)"), ubl[:, :, :].rearrange("p t n -> p (t n)")).then_inc(u_stored, 16)

                def load_u(b):
                    wait(u_stored, b * 16 + 16)
                    pool.dma_start(u8[:, :, :], scr_u.rearrange("c g t n -> t (c g) n")).then_inc(u8_in, 16)

                def build_toep(b):
                    wait(ka_ready, b + 1)
                    pool.dma_start(scr_k[:, :, P:2 * P], kam[:, :, :]).then_inc(k_stored, 16)
                    wait(k_stored, b * 16 + 32)
                    rows = scr_k.rearrange("c g x -> (c g) x")
                    src = bass.AP(tensor=rows.tensor, offset=SC, ap=[[SC, TAP], [2 * P, SC * 8], [1, P]])
                    pool.dma_start(toep[:, :, :], src).then_inc(toep_in, 16)

                def move_y(b, j, next_u=False):
                    wait(y8_ready, b + 2)
                    if next_u:
                        load_u(b + 1)
                    pool.dma_start(scr_y.rearrange("c t g n -> t c (g n)"), y8[:, :, :].rearrange("p g n -> p (g n)")).then_inc(y_stored, 16)
                    wait(y_stored, b * 16 + 16)
                    pool.dma_start(yfm[:, ds(j, 1), :].rearrange("p a (t n) -> p (a t) n", n=NCH), scr_y.rearrange("c t g n -> g (c t) n")).then_inc(yfm_in, 16)

                store_u(l * 4)
                load_u(l * 4)
                build_toep(l * 4)
                with pool.Fori(0, 3) as j:
                    b = l * 4 + j
                    store_u(b + 1)
                    move_y(b, j, True)
                    build_toep(b + 1)
                move_y(l * 4 + 3, 3)

        @block.tensor
        def _(pe):
            def products(bank, slot, blocks, hi, lo, first=True, last=True):
                for i, (blk, k) in enumerate(blocks):
                    wh = whi[:, slot, blk * P:blk * P + P]
                    wl = wlo[:, slot, blk * P:blk * P + P]
                    pe.matmul(ps[:, bank, :], wh, hi[:, k, :], start=first and i == 0, stop=False)
                    pe.matmul(ps[:, bank, :], wh, lo[:, k, :], start=False, stop=False)
                    m = pe.matmul(ps[:, bank, :], wl, hi[:, k, :], start=False, stop=last and i == len(blocks) - 1)
                return m

            def x_slab(h, c, bank, freed, o, x_before=None):
                pe.wait_ge(lo_ready, h * 2 + (c + 3))
                pe.wait_ge(freed, o)
                for k in range(KD):
                    if x_before is not None and k % 2 == 0:
                        pe.wait_ge(x_ready, x_before + (k // 2 + 1))
                    m = products(bank, c % 2, [(k, k)], xh, xl, k == 0, k == KD - 1)
                m.then_inc(slab_done, 1)

            ident = cnv("ident")
            with pe.Fori(0, L) as l:
                hl_ = l * (NSLAB // 2)
                ao = l * ACT_OUTS
                do = l * DVE_OUTS
                with pe.Fori(0, NA1 // 2) as i:
                    for c in range(2):
                        pe.wait_ge(dve_out_freed, do + 4)
                        x_slab(hl_ + i, c, c, act_out_freed, ao + i * 2 + (c + 1), l * 8 if c == 0 else None)
                pe.wait_ge(small_in, l * 16 + 16)
                wg = smv("wg", KD, 24)
                for k in range(KD):
                    m = pe.matmul(ps[0:24, 7, :], wg[:, k, :], xf[:, k, :], start=k == 0, stop=k == KD - 1)
                m.then_inc(qgate_psum, 1)
                pe.wait_ge(consts_in, 48)
                for i in (2, 0, 1):
                    pe.wait_ge(act_out_freed, ao + 2 + 3)
                    pe.matmul(ps[:, 4 + i, :], cnv("rot"), pa[:, i, :], start=True, stop=True).then_inc(krot_psum, 1)
                pe.wait_ge(act_out_freed, ao + 2 + 6)
                for v in range(2):
                    for t in range(4):
                        m = pe.transpose(ps[:, 2 + v, P * t:P * t + P], pa[:, 4 + v, P * t:P * t + P], ident)
                    m.then_inc(vtok_psum, 1)
                def a2_slab(i):
                    x_slab(hl_ + (OA2 + i - i % 2) // 2, i % 2, i % 2, act_out_freed, ao + OA2 + (i + 1))

                pe.wait_ge(qgate_tanh, l + 1)
                a2_slab(0)
                for t in range(4):
                    m = pe.transpose(ps[:, 7, 24 * t:24 * t + 24], gqt[:, P * t:P * t + P], ident[0:24, 0:24])
                m.then_inc(qgate_tok, 1)
                a2_slab(1)
                for n, j in enumerate((1, 0)):
                    pe.wait_ge(z_ready, l * 2 + (n + 1))
                    pe.wait_ge(w1_in[j], (l + 1) * 16)
                    if n == 0:
                        pe.wait_ge(krot_done, l * 3 + 3)
                    for t in range(16):
                        m = pe.matmul(ps[0:2 * NCMP, 4, CH * j:CH * j + CH], zb[:, j, t, :, :].rearrange("p h n -> p (h n)"),
                                      w1[:, j, t * CH:t * CH + CH], start=t == 0, stop=t == 15)
                m.then_inc(hid_tok, 1)
                a2_slab(2)

                def s5_mats(b):
                    pe.wait_ge(mats_ready, b + 1)
                    for q in range(2):
                        for g in range(4):
                            m = pe.transpose(ps[:, 4 + q, P * g:P * g + P], vmat[:, q, g, :], ident)
                    m.then_inc(vt_psum, 1)
                    for par in range(2):
                        rows = slice(64 * par, 64 * par + 64)
                        for g in range(4):
                            for q in range(2):
                                m = pe.matmul(ps[0:SC, 2 + par, P * g:P * g + P], bch[rows, q, g, :], wmat[rows, q, g, 0:P],
                                              start=q == 0, stop=q == 1)
                    m.then_inc(ka_psum, 1)

                def s5_chunk(b, h, j):
                    pe.wait_ge(vt_ready, b + 1)
                    pe.wait_ge(u8_in, b * 16 + 16)
                    for q in range(2):
                        for g in range(8):
                            par, gp = g % 2, g // 2
                            m = pe.matmul(ps[64 * par:64 * par + 64, 4, (4 * q + gp) * NCH:(4 * q + gp + 1) * NCH],
                                          vt[:, q, gp, 64 * par:64 * par + 64], u8[:, g, :], start=True, stop=True)
                    m.then_inc(x_state_psum, 1)
                    x_slab(h, 0, 0, act_out_freed, ao + OB1 + j * 2 + 1)
                    pe.wait_ge(toep_in, b * 16 + 16)
                    pe.wait_ge(h_ready, b + 1)
                    pe.wait_ge(kc_ready, l + 1)
                    pe.wait_ge(y8_ready, b + 1)
                    for par in range(2):
                        rows = slice(64 * par, 64 * par + 64)
                        for gp in range(4):
                            o = ps[:, 6 + par, gp * NCH:(gp + 1) * NCH]
                            pe.matmul(o, toep[:, 2 * gp + par, :], u8[:, 2 * gp + par, :], start=True, stop=False)
                            pe.matmul(o, wmat[rows, 0, gp, SC:9 * SC], hst[rows, 0, gp, 0:NCH], start=False, stop=False)
                            m = pe.matmul(o, wmat[rows, 1, gp, SC:9 * SC], hst[rows, 1, gp, 0:NCH], start=False, stop=True)
                    m.then_inc(y_psum, 1)
                    x_slab(h, 1, 1, act_out_freed, ao + OB1 + j * 2 + 2)

                pe.wait_ge(vtok_ready, l + 1)
                pe.wait_ge(hid_copied, l + 1)
                s5_mats(l * 4)
                for i in range(4):
                    m = pe.transpose(ps[:, 6, 2 * NCMP * i:2 * NCMP * i + 2 * NCMP], hidt[:, P * i:P * i + P], ident[0:2 * NCMP, 0:2 * NCMP])
                m.then_inc(hid_psum, 1)
                a2_slab(3)
                pe.wait_ge(qgate_taken, l + 1)
                pe.wait_ge(hid_ready, l + 1)
                w2 = smv("w2", 4, HD)
                for h in range(2):
                    for m2 in range(2):
                        pe.matmul(ps[64 * h:64 * h + 64, 6, 0:NCMP], w2[:, m2, :], hgt[:, m2, NCMP * h:NCMP * h + NCMP],
                                  start=m2 == 0, stop=m2 == 1)
                for h in range(2):
                    for m2 in range(2):
                        m = pe.matmul(ps[0:NCMP, 7, HD * h:HD * h + HD], hgt[:, 2 + m2, NCMP * h:NCMP * h + NCMP], w2[:, 2 + m2, :],
                                      start=m2 == 0, stop=m2 == 1)
                m.then_inc(kc_psum, 1)
                with pe.Fori(0, 3) as j:
                    s5_chunk(l * 4 + j, hl_ + OB1 // 2 + j, j)
                    s5_mats(l * 4 + j + 1)
                s5_chunk(l * 4 + 3, hl_ + OB1 // 2 + 3, 3)
                with pe.Fori(0, 4) as j:
                    b = l * 4 + j
                    h = hl_ + OB2 // 2 + j * 2

                    def slab(c):
                        x_slab(h, c, (0, 1, 0, 6)[c], act_out_freed, ao + OB2 + j * 4 + (c + 1))

                    slab(0)
                    slab(1)
                    pe.wait_ge(act_out_freed, ao + OB2 + j * 4 + 3)
                    pe.wait_ge(y8_ready, l * 4 + 5)
                    pe.matmul(ps[:, 6, :], cnv("rot"), qraw[:, :], start=True, stop=True).then_inc(q_rot_psum, 1)
                    slab(2)
                    pe.wait_ge(q_ready, b + 2)
                    for kv in range(2):
                        rows = slice(64 * kv, 64 * kv + 64)
                        for t in range(4):
                            m = pe.matmul(ps[:, 2 + kv, NCMP * t:NCMP * t + NCMP], qro[rows, P * t:P * t + P], kct[rows, :],
                                          start=True, stop=True)
                    m.then_inc(cs_psum, 1)

                    def scores(s):
                        kv, t = s // 4, s % 4
                        rows = slice(64 * kv, 64 * kv + 64)
                        n = P * (t + 1)
                        for br in range(2):
                            m = pe.matmul(ps[:, sbank(s) + br, 0:n], qro[rows, P * t:P * t + P], kro[rows, br, 0:n], start=True, stop=False)
                        for br in range(2):
                            m = pe.matmul(ps[:, sbank(s) + br, P * t:n], ident, cnv("dmask"), start=False, stop=True)
                        m.then_inc(s_psum, 1)

                    scores(0)
                    pe.wait_ge(act_out_freed, ao + OB2 + j * 4 + 5)
                    scores(1)
                    slab(3)
                    pe.wait_ge(cs_ready, b + 1)
                    for i in range(8):
                        m = pe.transpose(ps[0:NCMP, 2 + i // 4, P * (i % 4):P * (i % 4) + P], pc[:, i, :], ident)
                    m.then_inc(cs_tpsum, 1)
                    pe.wait_ge(s_exp, b * 8 + 1)
                    scores(2)
                    for s in range(8):
                        kv, t = s // 4, s % 4
                        if s == 0:
                            pe.wait_ge(cs_tready, b + 1)
                        for br, scaled in ((0, p_sel), (1, p_win)):
                            pe.wait_ge(scaled, b * 8 + (s + 1))
                            for k in range(t + 1):
                                m = pe.transpose(ps[:, 2 + br, P * k:P * k + P], prob[:, s % 3, br, P * k:P * k + P], ident)
                        m.then_inc(s_tpsum, 1)
                        if s < 5:
                            pe.wait_ge(s_exp, b * 8 + (s + 2))
                            scores(s + 3)
                        o = ps[64 * kv:64 * kv + 64, 7, P * t:P * t + P]
                        if s == 0:
                            pe.wait_ge(o_ready, b + 1)
                        pe.matmul(o, vct[0:NCMP, kv, :], pct[0:NCMP, s, :], start=True, stop=False)
                        for br, there in ((1, pt_win), (0, pt_sel)):
                            pe.wait_ge(there, b * 8 + (s + 1))
                            for k in range(t + 1):
                                m = pe.matmul(o, vtok[:, br, k, 64 * kv:64 * kv + 64], probt[:, s % 2, br, P * k:P * k + P],
                                              start=False, stop=br == 0 and k == t)
                        m.then_inc(o_psum, 1)
                wp = smv("wpool", 4, P)
                pe.wait_ge(pool_ready, l + 1)
                for g in range(4):
                    if g == 3:
                        pe.wait_ge(o_ready, l * 4 + 5)
                    src = (pla if g % 2 == 0 else plb)[:, g, :]
                    pe.matmul(ps[:, 4 + g, :], wp[:, g, :], src, start=True, stop=True).then_inc(mix_psum, 1)
                four = [(k, k) for k in range(4)]
                four_up = [(4 + k, k) for k in range(4)]
                with pe.Fori(0, NGL // 2) as i:
                    h = hl_ + OGL // 2 + i
                    pe.wait_ge(ys_ready, l * 4 + 4)
                    pe.wait_ge(act_out_freed, ao + ACT_OUTS + 2)
                    for c in range(2):
                        pe.wait_ge(lo_ready, h * 2 + (c + 3))
                        pe.wait_ge(dve_out_freed, do + DGL + i * 4 + (2 * c + 2))
                        products(2 * c, c, four, ysh, ysl)
                        products(2 * c + 1, c, four_up, ysh, ysl).then_inc(slab_done, 1)
                with pe.Fori(0, 2) as i:
                    pe.wait_ge(glu_ready, l * 4 + 4)
                    pe.wait_ge(mix_ready, l * 4 + 5)
                    for c in range(10):
                        q = c % 5
                        h = hl_ + OC // 2 + i * 5
                        first = do + DC + i * 16 + (8 * (c // 5))
                        bank = (0, 2, 0, 1, 2)[q]
                        if q in (2, 3):
                            x_slab(h, c, bank, dve_out_freed, first + (4 + (q - 2) + 1))
                            continue
                        pe.wait_ge(lo_ready, h * 2 + (c + 3))
                        if q == 0:
                            pe.wait_ge(mg_tanh, l * 4 + i * 2 + (c // 5 + 1))
                        else:
                            pe.wait_ge(dve_out_freed, first + {1: 4, 4: 8}[q])
                        hi, lo = {0: (glh, gll), 1: (plh, pll), 4: (nsh, nsl)}[q]
                        products(bank, c % 2, four, hi, lo)
                        products(bank + 1, c % 2, four_up, hi, lo).then_inc(slab_done, 1)

                def to_tokens(rbuf, m, count):
                    pe.wait_ge(r_ready, count + 1)
                    pe.wait_ge(stats_done, count + 1)
                    for t in range(4):
                        x = pe.transpose(ps[:, 4 + m % 2, P * t:P * t + P], rbuf[:, m, P * t:P * t + P], ident)
                    x.then_inc(rt_psum, 1)

                def spread(n):
                    pe.wait_ge(ln_bc, n + 1)
                    for w in range(2):
                        for t in range(4):
                            x = pe.transpose(ps[:, 6 + w, P * t:P * t + P], lnbc[:, w, t, :], ident)
                    x.then_inc(ln_psum, 1)

                for c in range(NO):
                    pe.wait_ge(lo_ready, (hl_ + OO // 2) * 2 + (c + 3))
                    pe.wait_ge(dve_out_freed, do + DO + (c + 1))
                    for k in range(KD):
                        if c == 0 and k % 2 == 0:
                            pe.wait_ge(mg_ready, l * 4 + (k // 2 + 1))
                        m = products(c % 4, c % 2, [(k, k)], mgh, mgl, k == 0, k == KD - 1)
                    m.then_inc(slab_done, 1)
                    if c:
                        to_tokens(r1, c - 1, l * 16 + (c - 1))
                to_tokens(r1, NO - 1, l * 16 + (NO - 1))
                spread(l * 2)
                with pe.Fori(0, NF // 4) as i:
                    for c in range(4):
                        h = hl_ + OF // 2 + i * 2
                        x_slab(h, c, c, dve_out_freed, do + DF + i * 4 + (c + 1), l * 8 + 4 if c == 0 else None)
                def two_outputs(i, first=False):
                    for o in range(2):
                        for q in range(3):
                            c = 3 * o + q
                            pe.wait_ge(lo_ready, (hl_ + OG // 2 + i * 3) * 2 + (c + 3))
                            pe.wait_ge(ff_ready, l * KF + min(8 * q + 8, KF))
                            if q == 0:
                                pe.wait_ge(dve_out_freed, do + DG + (2 if first else i * 2 + (o + 3)))
                            blocks = [(k, 8 * q + k) for k in range(min(8, KF - 8 * q))]
                            products(o, c % 2, blocks, hh, hl, q == 0, q == 2).then_inc(slab_done, 1)
                            if q == 0 and o == 1:
                                to_tokens(rst, 0, l * 16 + 8 + i * 2)
                            if q == 0 and o == 0 and not first:
                                to_tokens(rst, 1, l * 16 + 7 + i * 2)

                two_outputs(0, True)
                with pe.Fori(0, 3) as i:
                    two_outputs(i + 1)
                to_tokens(rst, 1, l * 16 + 15)
                spread(l * 2 + 1)

        @block.scalar
        def _(act):
            def split_hi(h, c):
                act.wait_ge(raw_loaded[c % 2], (h + (c // 2 + 1)) * 16)
                act.wait_ge(slab_done, h * 2 + (c + 1))
                act.activation(whi[:, c % 2, :], raw[:, c % 2, :], ACT.Copy).then_inc(hi_ready, 1)

            def slab_out(h, c):
                act.wait_ge(slab_done, h * 2 + (c + 3))

            def ln_part(rbuf, l, w, n):
                act.wait_ge(var_ready, n + 1)
                act.activation(lnrs[:, :], lnrs[:, :], ACT.Sqrt).then_inc(sd_ready, 1)
                for g in range(4):
                    act.wait_ge(ln_norm, n * 4 + (g + 1))
                    for m in (2 * g, 2 * g + 1):
                        gain = nrm[:, ds(l, 1), 16 * w + m]
                        shift = nrm[:, ds(l, 1), 16 * w + 8 + m]
                        act.activation(xh[:, m, :], rbuf[:, m, :], ACT.Identity, bias=shift, scale=gain)
                        x = act.activation(rbuf[:, m, :], rbuf[:, m, :], ACT.Identity, bias=shift, scale=gain)
                    x.then_inc(ln_x, 1)

            for g in range(4):
                act.dma_start(xf[:, 2 * g:2 * g + 2, :], xin[:, 2 * g:2 * g + 2, :]).then_inc(x_in[g], 16)
            for g in range(4):
                act.wait_ge(x_in[g], 16)
                act.activation(xh[:, 2 * g:2 * g + 2, :], xf[:, 2 * g:2 * g + 2, :], ACT.Copy).then_inc(x_hi, 1)
                if g == 0:
                    split_hi(0, 0)
            act.wait_ge(rope_arg, 1)
            act.activation(sin_t[:, :], sin_t[:, :], ACT.Sin)
            act.activation(cos_t[:, :], cos_t[:, :], ACT.Sin).then_inc(rope_done, 1)
            with act.Fori(0, L) as l:
                hl_ = l * (NSLAB // 2)
                def a1_split(i):
                    split_hi(hl_ + i // 2, i % 2 + 1)

                def a1_out(i):
                    slab_out(hl_ + i // 2, i % 2)
                    act.activation(pa[:, i, :], ps[:, i % 2, :], ACT.Copy).then_inc(act_out_freed, 1)

                a1_split(0)
                act.wait_ge(small_in, l * 16 + 16)
                act.activation(st[:, 0, :], smv("ldt"), ACT.Exp).then_inc(dt_ready, 1)
                a1_out(0)
                a1_split(1)
                a1_out(1)
                a1_split(2)
                act.wait_ge(angle_ready, l + 1)
                for t in range(9):
                    act.activation(rp[:, t, :], st[:, 1, :], ACT.Exp, scale=float(t))
                act.activation(php[:, 1, 1, :], st[:, 2, :], ACT.Sin)
                act.activation(php[:, 0, 1, :], st[:, 3, :], ACT.Sin).then_inc(sincos_ready, 1)
                for i in range(2, NA1):
                    a1_out(i)
                    if i < NA1 - 1:
                        a1_split(i + 1)
                act.wait_ge(qgate_psum, l + 1)
                act.activation(gqt[:, :], ps[0:24, 7, :], ACT.Tanh, scale=0.5).then_inc(qgate_tanh, 1)
                act.wait_ge(vtok_psum, l * 2 + 2)
                act.activation(vtok[:, :, :, :].rearrange("p v t d -> p (v t d)"), ps[:, 2:4, :].rearrange("p b n -> p (b n)"), ACT.Copy)\
                   .then_inc(vtok_ready, 1)

                def a2_split(i):
                    split_hi(hl_ + (OA2 + i - i % 2) // 2, i % 2 + 1)

                def a2_out(i):
                    slab_out(hl_ + (OA2 + i - i % 2) // 2, i % 2)
                    act.activation(pa[:, 6 + i, :], ps[:, i % 2, :], ACT.Copy).then_inc(act_out_freed, 1)

                a2_split(0)
                a2_out(0)
                a2_split(1)
                a2_out(1)
                a2_split(2)
                act.wait_ge(hid_tok, l + 1)
                act.activation(hidt[:, :], ps[0:2 * NCMP, 4, :], ACT.Copy).then_inc(hid_copied, 1)
                a2_out(2)

                def s5_mats(b):
                    act.wait_ge(vt_psum, b + 1)
                    act.activation(vt[:, :, :, :].rearrange("p q g n -> p (q g n)"), ps[:, 4:6, :].rearrange("p b n -> p (b n)"), ACT.Copy)\
                       .then_inc(vt_ready, 1)
                    act.wait_ge(ka_psum, b + 1)
                    for par in range(2):
                        x = act.activation(kam[:, :, :].rearrange("p (g q) n -> p q g n", q=2)[:, par, :, :],
                                           ps[0:SC, 2 + par, :].rearrange("p (g n) -> p g n", g=4), ACT.Copy)
                    x.then_inc(ka_copied, 1)

                def s5_chunk(b, h, j):
                    split_hi(h, 1)
                    slab_out(h, 0)
                    act.activation(upool[:, ds(j, 1), :].rearrange("p a n -> p (a n)"), ps[:, 0, :], ACT.Copy).then_inc(act_out_freed, 1)
                    split_hi(h, 2)
                    act.wait_ge(y_psum, b + 1)
                    for par in range(2):
                        x = act.activation(y8[:, :, :].rearrange("p (g q) n -> p q g n", q=2)[:, par, :, :],
                                           ps[:, 6 + par, 0:4 * NCH].rearrange("p (g n) -> p g n", g=4), ACT.Copy)
                    x.then_inc(y8_ready, 1)
                    slab_out(h, 1)
                    act.activation(gates[:, ds(j, 1), :].rearrange("p a n -> p (a n)"), ps[:, 1, :], ACT.Tanh, scale=0.5).then_inc(act_out_freed, 1)

                a2_split(3)
                s5_mats(l * 4)
                act.wait_ge(hid_psum, l + 1)
                b1 = smv("b1")
                for i in range(4):
                    x = act.activation(hid[:, i, :], ps[:, 6, 2 * NCMP * i:2 * NCMP * i + 2 * NCMP], ACT.Identity, bias=b1[:, i:i + 1])
                x.then_inc(hid_biased, 1)
                act.wait_ge(gelu_arg, l * 5 + 1)
                act.activation(hgt[:, :, :], hgt[:, :, :], ACT.Tanh, scale=GELU_B).then_inc(gelu_tanh, 1)
                a2_out(3)
                act.wait_ge(kc_psum, l + 1)
                with act.Fori(0, 3) as j:
                    s5_chunk(l * 4 + j, hl_ + OB1 // 2 + j, j)
                    s5_mats(l * 4 + j + 1)
                s5_chunk(l * 4 + 3, hl_ + OB1 // 2 + 3, 3)
                with act.Fori(0, 4) as j:
                    b = l * 4 + j
                    h = hl_ + OB2 // 2 + j * 2
                    split_hi(h, 1)
                    slab_out(h, 0)
                    act.wait_ge(q_ready, b + 1)
                    act.activation(qraw[:, :], ps[:, 0, :], ACT.Copy, scale=SCALE).then_inc(act_out_freed, 1)

                    def gate(c):
                        slab_out(h, c)
                        act.activation(gates[:, ds(j * 3 + (3 + c), 1), :].rearrange("p a n -> p (a n)"), ps[:, c % 2, :], ACT.Tanh, scale=0.5)\
                           .then_inc(act_out_freed, 1)

                    split_hi(h, 2)
                    gate(1)
                    act.wait_ge(gelu_arg, l * 5 + j + 2)
                    act.activation(ygt[:, :], ygt[:, :], ACT.Tanh, scale=GELU_B).then_inc(gelu_tanh, 1)
                    act.wait_ge(ygelu_ready, b + 1)
                    act.activation(ysh[:, ds(j, 1), :].rearrange("p a (n t) -> p (a n) t", t=TAP), ygt[:, :].rearrange("p (t n) -> p n t", n=NCH), ACT.Copy, scale=0.5)\
                       .then_inc(ys_hi, 1)
                    split_hi(h, 3)
                    gate(2)
                    act.wait_ge(cs_shift, b + 1)
                    act.activation(pc[:, :, :], pc[:, :, :], ACT.Exp).then_inc(cs_exp, 1)

                    def exps(s):
                        n = P * (s % 4 + 1)
                        act.wait_ge(s_max, b * 8 + (s + 1))
                        for br in range(2):
                            x = act.activation(prob[:, s % 3, br, 0:n], ps[:, sbank(s) + br, 0:n], ACT.Exp,
                                               bias=tiny[:, 28 + 8 * (s % 3) + br:29 + 8 * (s % 3) + br],
                                               accum_out=tiny[:, 30 + 8 * (s % 3) + br:31 + 8 * (s % 3) + br])
                        x.then_inc(s_exp, 1)

                    def scale(s):
                        n = P * (s % 4 + 1)
                        act.wait_ge(s_ratio, b * 8 + (s + 1))
                        act.activation(prob[:, s % 3, 0, 0:n], prob[:, s % 3, 0, 0:n], ACT.Copy, scale=tiny[:, 52 + 2 * (s % 3):53 + 2 * (s % 3)])\
                           .then_inc(p_sel, 1)

                    exps(0)
                    exps(1)
                    split_hi(h, 4)
                    slab_out(h, 3)
                    act.activation(gates[:, ds(j * 3 + 6, 1), :].rearrange("p a n -> p (a n)"), ps[:, 6, :], ACT.Tanh, scale=0.5)\
                       .then_inc(act_out_freed, 1)
                    scale(0)
                    act.wait_ge(cs_tpsum, b + 1)
                    act.activation(pct[0:NCMP, :, :].rearrange("p s n -> p (s n)"), ps[0:NCMP, 2:4, :].rearrange("p b n -> p (b n)"), ACT.Copy)\
                       .then_inc(cs_tready, 1)
                    exps(2)
                    for s in range(8):
                        n = P * (s % 4 + 1)
                        act.wait_ge(s_tpsum, b * 8 + (s + 1))
                        act.activation(probt[:, s % 2, 0, 0:n], ps[:, 2, 0:n], ACT.Copy).then_inc(pt_sel, 1)
                        if s < 7:
                            scale(s + 1)
                        if s < 5:
                            exps(s + 3)
                    act.wait_ge(o_psum, b * 8 + 8)
                    act.activation(nsh[:, ds(j, 1), :].rearrange("p a n -> p (a n)"), ps[:, 7, :], ACT.Copy).then_inc(o_hi, 1)
                for g in range(4):
                    act.wait_ge(mix_psum, l * 4 + (g + 1))
                    act.activation(plh[:, g, :], ps[:, 4 + g, :], ACT.Copy, scale=smv("psc")[:, g:g + 1]).then_inc(mix_hi, 1)
                with act.Fori(0, NGL // 2) as i:
                    h = hl_ + OGL // 2 + i
                    for c in range(2):
                        split_hi(h, c + 1)
                        slab_out(h, c)
                        act.activation(gt[:, :], ps[:, 2 * c + 1, :], ACT.Tanh, scale=0.5).then_inc(glu_tanh, 1)
                        act.wait_ge(glu_raw, l * 4 + i * 2 + (c + 1))
                        act.activation(glh[:, ds(i * 2 + c, 1), :].rearrange("p a n -> p (a n)"), gv[:, :], ACT.Copy, scale=0.5).then_inc(glu_hi, 1)
                with act.Fori(0, 2) as i:
                    for c in range(10):
                        h = hl_ + OC // 2 + i * 5
                        split_hi(h, c + 1)
                        if c % 5 == 3:
                            slab_out(h, c)
                            act.activation(tg2[:, :, :].rearrange("p b n -> p (b n)"), ps[:, 0:2, :].rearrange("p b n -> p (b n)"), ACT.Tanh, scale=0.5)\
                               .then_inc(mg_tanh, 1)
                        if c in (5, 9):
                            pr = 0 if c == 5 else 1
                            act.wait_ge(mg_raw, l * 4 + i * 2 + (pr + 1))
                            act.activation(mgh[:, ds(i * 4 + 2 * pr, 2), :], acc[:, :, :], ACT.Copy, scale=0.5).then_inc(mg_hi, 1)
                for c in range(NO):
                    split_hi(hl_ + OO // 2, c + 1)
                ln_part(r1, l, 0, l * 2)
                with act.Fori(0, NF // 4) as i:
                    h = hl_ + OF // 2 + i * 2
                    for c in range(4):
                        split_hi(h, c + 1)
                        if c % 2 == 0:
                            slab_out(h, c)
                            act.activation(ft[:, c // 2, :], ps[:, c, :], ACT.Tanh, scale=0.5).then_inc(ff_tanh, 1)
                        else:
                            act.wait_ge(ff_raw, l * KF + i * 2 + (c // 2 + 1))
                            act.activation(hh[:, ds(i * 2 + c // 2, 1), :].rearrange("p a n -> p (a n)"), fb[:, c // 2, :], ACT.Copy, scale=0.5)\
                               .then_inc(ff_hi, 1)
                with act.Fori(0, 4) as i:
                    h = hl_ + OG // 2 + i * 3
                    for o in range(2):
                        for q in range(3):
                            split_hi(h, 3 * o + q + 1)
                        act.wait_ge(r_ready, l * 16 + 8 + i * 2 + (o + 1))
                        act.activation(xf[:, ds(i * 2 + o, 1), :].rearrange("p a n -> p (a n)"), rst[:, o, :], ACT.Copy).then_inc(r_kept, 1)
                ln_part(xf, l, 1, l * 2 + 1)

        @block.vector
        def _(dve):
            def split_lo(h, c):
                dve.wait_ge(hi_ready, h * 2 + (c + 1))
                dve.tensor_tensor(wlo[:, c % 2, :], raw[:, c % 2, :], whi[:, c % 2, :].bitcast(f32), SUB).then_inc(lo_ready, 1)

            def slab_out(h, c):
                dve.wait_ge(slab_done, h * 2 + (c + 3))

            def tt(o, a, b, op):
                return dve.tensor_tensor(o, a, b, op)

            def cmul(orr, oi, ar, ai, br, bi, t1, t2, conj=False, neg_i=False):
                tt(t1, ar, br, MUL)
                tt(t2, ai, bi, MUL)
                dve.drain()
                tt(orr, t1, t2, ADD if conj else SUB)
                dve.drain()
                tt(t1, ar, bi, MUL)
                tt(t2, ai, br, MUL)
                dve.drain()
                if neg_i:
                    return dve.scalar_tensor_tensor(oi, t1, -1.0, t2, MUL, SUB)
                return tt(oi, t1, t2, SUB if conj else ADD)

            def cmul4(orr, oi, ar, ai, br, bi, t, conj=False):
                tt(t[0], ar, br, MUL)
                tt(t[1], ai, bi, MUL)
                tt(t[2], ar, bi, MUL)
                tt(t[3], ai, br, MUL)
                dve.drain()
                tt(orr, t[0], t[1], ADD if conj else SUB)
                return tt(oi, t[2], t[3], SUB if conj else ADD)

            def to_phase(x, co, k):
                dve.tensor_scalar(k, x, 1.0 / (2 * math.pi), MAGIC, MUL, ADD)
                dve.drain()
                dve.tensor_scalar(k, k, MAGIC, None, SUB)
                dve.drain()
                for part in (TWO_PI_1, TWO_PI_2, TWO_PI_3):
                    dve.scalar_tensor_tensor(x, k, -part, x, MUL, ADD)
                    dve.drain()
                dve.tensor_scalar(x, x, PI_F, -PI_F, MIN, MAX)
                dve.drain()
                dve.scalar_tensor_tensor(co, x, -1.0, x, MUL, MAX)
                dve.drain()
                return dve.tensor_scalar(co, co, -1.0, math.pi / 2, MUL, ADD)

            def gelu(y, t, n):
                tt(t, y, y, MUL)
                dve.drain()
                dve.tensor_scalar(t, t, GELU_A, 1.0, MUL, ADD)
                dve.drain()
                tt(t, t, y, MUL).then_inc(gelu_arg, 1)
                dve.wait_ge(gelu_tanh, n + 1)
                return dve.scalar_tensor_tensor(t, t, 1.0, y, ADD, MUL)

            def residual(dst, m, bank, x_m):
                dve.scalar_tensor_tensor(dst, xh[:, x_m, :].bitcast(f32), ALPHA, ps[:, bank, :], MUL, ADD).then_inc(dve_out_freed, 1)
                dve.drain()
                return dve.scalar_tensor_tensor(dst, xl[:, x_m, :].bitcast(f32), ALPHA, dst, MUL, ADD).then_inc(r_ready, 1)

            def stats(m, bank, count):
                dve.wait_ge(rt_psum, count + 1)
                for t in range(4):
                    x = dve.bn_stats(lnst[:, t, m, :], ps[:, bank, P * t:P * t + P])
                x.then_inc(stats_done, 1)

            def ln_part(rbuf, n):
                dve.drain()
                for t in range(4):
                    dve.bn_aggr(lnmv[:, t, :], lnst[:, t, :, :].rearrange("p m s -> p (m s)"))
                dve.drain()
                dve.tensor_scalar(lnrs[:, :], lnmv[:, :, 1], EPS, None, ADD).then_inc(var_ready, 1)
                dve.tensor_copy(lnbc[:, 0, :, :], bc(lnmv[:, :, 0], 2, P))
                dve.wait_ge(sd_ready, n + 1)
                dve.reciprocal(lnrs[:, :], lnrs[:, :])
                dve.drain()
                dve.tensor_copy(lnbc[:, 1, :, :], bc(lnrs[:, :], 2, P)).then_inc(ln_bc, 1)
                dve.wait_ge(ln_psum, n + 1)
                for g in range(5):
                    if g < 4:
                        v = rbuf[:, 2 * g:2 * g + 2, :]
                        tt(v, v, bc(ps[:, 6, :], 1, 2), SUB)
                        dve.drain()
                        tt(v, v, bc(ps[:, 7, :], 1, 2), MUL).then_inc(ln_norm, 1)
                    if g:
                        dve.wait_ge(ln_x, n * 4 + g)
                        tt(xl[:, 2 * g - 2:2 * g, :], rbuf[:, 2 * g - 2:2 * g, :], xh[:, 2 * g - 2:2 * g, :].bitcast(f32), SUB).then_inc(x_ready, 1)

            dve.memset(tiny[:, 0:1], 0.0).then_inc(lo_ready, 2)
            dve.memset(tiny[:, 1:2], 0.0).then_inc(slab_done, 2)
            dve.memset(tiny[:, 2:3], 0.0).then_inc(act_out_freed, 2)
            dve.memset(tiny[:, 3:4], 0.0).then_inc(dve_out_freed, 4)
            dve.memset(tiny[:, 4:5], 0.0).then_inc(stats_done, 2)
            dve.memset(tiny[:, 5:6], 0.0).then_inc(o_ready, 1)
            dve.memset(tiny[:, 6:7], 0.0).then_inc(mix_ready, 1)
            dve.memset(tiny[:, 7:8], 0.0).then_inc(y8_ready, 1)
            dve.memset(tiny[:, 8:9], 0.0).then_inc(q_ready, 1)
            dve.memset(tiny[:, 9:10], 0.0).then_inc(mg_tanh, 1)
            def rotations():
                dve.wait_ge(consts_in, 48)
                dve.tensor_copy(kro[:, 1, :], kro[:, 0, :].bitcast(i32))
                dve.drain()
                dve.tensor_scalar(sin_t[:, :], kro[:, 1, :], cnv("inv"), None, MUL)
                dve.drain()
                to_phase(sin_t[:, :], cos_t[:, :], kro[:, 1, :]).then_inc(rope_arg, 1)

            for g in range(4):
                dve.wait_ge(x_hi, g + 1)
                v = slice(2 * g, 2 * g + 2)
                tt(xl[:, v, :], xf[:, v, :], xh[:, v, :].bitcast(f32), SUB).then_inc(x_ready, 1)
                if g == 0:
                    split_lo(0, 0)
                if g == 1:
                    rotations()

            with dve.Fori(0, L) as l:
                hl_ = l * (NSLAB // 2)
                ao = l * ACT_OUTS
                def a1_lo(i):
                    split_lo(hl_ + i // 2, i % 2 + 1)

                a1_lo(0)
                dve.wait_ge(dt_ready, l + 1)
                are, aim = smv("are"), smv("aim")
                tt(st[:, 1, :], are, st[:, 0, :], MUL)
                tt(st[:, 2, :], aim, st[:, 0, :], MUL)
                dve.drain()
                to_phase(st[:, 2, :], st[:, 3, :], st[:, 4, :]).then_inc(angle_ready, 1)
                a1_lo(1)
                a1_lo(2)
                dve.memset(php[:, 0, 0, :], 1.0)
                dve.memset(php[:, 1, 0, :], 0.0)
                dve.memset(hst[:, :, :, 0:1], 0.0)
                dve.memset(eph[:, 0, :, 0:1], 1.0)
                dve.memset(eph[:, 1, :, 0:1], 0.0)
                dve.wait_ge(sincos_ready, l + 1)
                for w in (1, 2, 4):
                    lo, n = slice(1, w + 1), slice(w + 1, 2 * w + 1)
                    pr, pi = bc(php[:, 0, w, :], 1, w), bc(php[:, 1, w, :], 1, w)
                    cmul(php[:, 0, n, :], php[:, 1, n, :], php[:, 0, lo, :], php[:, 1, lo, :], pr, pi, lam[:, 0, lo, :], lam[:, 1, lo, :])
                    dve.drain()
                tt(lam[:, 0, :, :], php[:, 0, :, :], rp[:, :, :], MUL)
                tt(lam[:, 1, :, :], php[:, 1, :, :], rp[:, :, :], MUL)
                dve.drain()
                a1_lo(3)
                dve.tensor_scalar(st[:, 5, :], lam[:, 0, 1, :], 1.0, None, SUB)
                tt(st[:, 6, :], are, are, MUL)
                tt(st[:, 7, :], aim, aim, MUL)
                dve.drain()
                tt(st[:, 6, :], st[:, 6, :], st[:, 7, :], ADD)
                dve.drain()
                dve.reciprocal(st[:, 6, :], st[:, 6, :])
                cmul(st[:, 8, :], st[:, 9, :], are, aim, st[:, 5, :], lam[:, 1, 1, :], st[:, 10, :], st[:, 11, :], conj=True)
                dve.drain()
                tt(coef[:, 0, :], st[:, 8, :], st[:, 6, :], MUL)
                tt(coef[:, 1, :], st[:, 9, :], st[:, 6, :], MUL)
                dve.tensor_copy(eph[:, :, :, 1], php[:, :, 8, :])
                dve.drain()

                def phasors(w, upto):
                    while 2 * w < upto:
                        cmul(st[:, 12, :], st[:, 13, :], eph[:, 0, :, w], eph[:, 1, :, w], eph[:, 0, :, w], eph[:, 1, :, w], st[:, 14, :], st[:, 15, :])
                        dve.drain()
                        w *= 2
                        old, new = slice(0, w), slice(w, 2 * w)
                        t1 = r8m[:, :, 0:w]
                        t2 = r8m[:, :, w:2 * w]
                        cmul(eph[:, 0, :, new], eph[:, 1, :, new], eph[:, 0, :, old], eph[:, 1, :, old],
                             bc(st[:, 12, :], 2, w), bc(st[:, 13, :], 2, w), t1, t2)
                        dve.drain()

                phasors(1, 8)
                a1_lo(4)
                phasors(4, NCH)
                dve.tensor_copy(r8m[:, :, :], bc(rp[:, 8, :], 2, NCH))
                dve.drain()
                dve.memset(r8m[:, :, 0:1], 0.0)
                dve.wait_ge(act_out_freed, ao + 2 + 4)
                dve.tensor_copy(zpm[:, 1, :, :].rearrange("p e m -> p m e"), pa[:, 3, :].rearrange("p (m e) -> p m e", e=2)).then_inc(z_perm, 1)
                a1_lo(5)
                dve.wait_ge(rope_done, 1)
                for n, i in enumerate((2, 0, 1)):
                    dve.wait_ge(krot_psum, l * 3 + (n + 1))
                    tt(rt1[:, :], pa[:, i, :], cos_t[:, :], MUL)
                    tt(rt2[:, :], ps[:, 4 + i, :], sin_t[:, :], MUL)
                    dve.drain()
                    if i < 2:
                        tt(kro[:, i, :], rt1[:, :], rt2[:, :], ADD).then_inc(krot_done, 1)
                    else:
                        v = "p (m e) -> p m e"
                        tt(zpm[:, 0, :, :].rearrange("p e m -> p m e"), rt1[:, :].rearrange(v, e=2), rt2[:, :].rearrange(v, e=2), ADD)\
                            .then_inc(krot_done, 1)
                    dve.drain()
                    if i == 2:
                        dve.memset(tiny[:, 0:1], 0.0).then_inc(z_perm, 1)

                def a2_lo(i):
                    split_lo(hl_ + (OA2 + i - i % 2) // 2, i % 2 + 1)

                a2_lo(0)
                a2_lo(1)
                def blocks_of(j):
                    for t in range(TAP):
                        u = pa[:, ds(j + 6, 1), :].rearrange("p a (n t) -> p (a t) n", t=TAP)[:, TAP - 1 - t, :]
                        x = dve.tensor_copy(ubl[:, t, :], u)
                    x.then_inc(ubl_ready, 1)

                def par_c(name, j):
                    return smv(name, GP, SC)[:, ds(j * 4, 4), :]

                def over(tab, q, n, j):
                    return tab[:, q, 0:n, ds(j * 4, 4)].rearrange("p t g -> p g t").unsqueeze(3).to_broadcast([P, 4, n, SC])

                def taps(x, n):
                    return x.unsqueeze(2).to_broadcast([P, 4, n, SC])

                v4 = "p (g t c) -> p g t c"

                def input_mats(j):
                    dve.drain()
                    t1, t2 = ta[:, 0:64].rearrange("p (g c) -> p g c", g=4), tb[:, 0:64].rearrange("p (g c) -> p g c", g=4)
                    cmul(bch[:, 0, :, :], bch[:, 1, :, :], bc(coef[:, 0, ds(j * 4, 4)], 2, SC), bc(coef[:, 1, ds(j * 4, 4)], 2, SC),
                         par_c("bre", j), par_c("bim", j), t1, t2)
                    dve.drain()
                    t1, t2 = ta[:, 0:512].rearrange(v4, g=4, c=SC), tb[:, 0:512].rearrange(v4, g=4, c=SC)
                    cmul(vmat[:, 0, :, :].rearrange("p g (t c) -> p g t c", c=SC), vmat[:, 1, :, :].rearrange("p g (t c) -> p g t c", c=SC),
                         over(lam, 0, 8, j), over(lam, 1, 8, j), taps(bch[:, 0, :, :], 8), taps(bch[:, 1, :, :], 8), t1, t2)

                def output_mats(j):
                    t1, t2 = ta[:, :].rearrange(v4, g=4, c=SC), tb[:, :].rearrange(v4, g=4, c=SC)
                    cmul(wmat[:, 0, :, :].rearrange("p g (t c) -> p g t c", c=SC), wmat[:, 1, :, :].rearrange("p g (t c) -> p g t c", c=SC),
                         over(lam, 0, 9, j), over(lam, 1, 9, j), taps(par_c("cre", j), 9), taps(par_c("cim", j), 9), t1, t2, neg_i=True).then_inc(mats_ready, 1)
                def skips(j):
                    tt(skip[:, :, :], bc(cnv("ident")[0:SC, 0:SC], 1, 8), bc(smv("dsk")[0:SC, ds(j * 8, 8)], 2, SC), MUL)
                    dve.drain()

                def add_skip(b):
                    dve.wait_ge(ka_copied, b + 1)
                    tt(kam[:, :, 0:SC], kam[:, :, 0:SC], skip[:, :, :], ADD).then_inc(ka_ready, 1)

                dve.wait_ge(qgate_tok, l + 1)
                dve.tensor_scalar(gq[:, :, :].rearrange("p t c -> p (t c)"), ps[:, 7, 0:96], 1.0, 0.5, ADD, MUL).then_inc(qgate_taken, 1)
                dve.wait_ge(act_out_freed, ao + 2 + (OA2 + 1))
                blocks_of(0)
                for j in (1, 0):
                    dve.wait_ge(z2_in[j], (l + 1) * 64)
                    for a in range(2):
                        x = tt(zb[:, j, 8 * a:8 * a + 8, :, :], z2[:, j, :, 8 * a:8 * a + 8 * NCMP].rearrange("p h (n t) -> p t h n", t=8),
                               smv("pos")[:, 16 * j + 8 * a:16 * j + 8 * a + 8].unsqueeze(2).unsqueeze(3).to_broadcast([P, 8, 2, NCMP]), ADD)
                    x.then_inc(z_ready, 1)
                a2_lo(2)
                input_mats(0)
                dve.drain()
                output_mats(0)
                dve.wait_ge(hid_biased, l + 1)
                gelu(hid[:, :, :], hgt[:, :, :], l * 5).then_inc(hid_ready, 1)
                a2_lo(3)
                skips(0)
                add_skip(l * 4)
                dve.wait_ge(kc_psum, l + 1)
                dve.tensor_scalar(kct[:, :], ps[:, 6, 0:NCMP], 0.5, None, MUL)
                dve.tensor_scalar(vct[0:NCMP, :, :].rearrange("p h d -> p (h d)"), ps[0:NCMP, 7, 0:2 * HD], 0.5, None, MUL).then_inc(kc_ready, 1)

                def s5_chunk(b, h, j, last):
                    split_lo(h, 1)
                    g4 = ds(j * 4, 4)
                    dve.wait_ge(x_state_psum, b + 1)
                    xs = [ps[:, 4, 4 * NCH * q:4 * NCH * (q + 1)] for q in range(2)]
                    er, ei = (eph[:, q, g4, :].rearrange("p g n -> p (g n)") for q in range(2))
                    sr, si = (srot[:, q, :, :].rearrange("p g n -> p (g n)") for q in range(2))
                    temps = [x[:, a:a + 256] for x in (ta, tb) for a in (0, 256)]
                    cmul4(sr, si, er, ei, xs[0], xs[1], temps, conj=True)
                    dve.drain()
                    for q in range(2):
                        dve.tensor_tensor_scan(gsc[:, q, :, :].rearrange("p g n -> p (g n)"), r8m[:, g4, :].rearrange("p g n -> p (g n)"),
                                               srot[:, q, :, :].rearrange("p g n -> p (g n)"), 0.0, MUL, ADD)
                    dve.drain()
                    v3 = "p (g n) -> p g n"
                    cmul4(hst[:, 0, :, 1:NCH + 1], hst[:, 1, :, 1:NCH + 1], eph[:, 0, g4, :], eph[:, 1, g4, :], gsc[:, 0, :, :], gsc[:, 1, :, :],
                          [x.rearrange(v3, g=4) for x in temps]).then_inc(h_ready, 1)
                    if not last:
                        dve.wait_ge(act_out_freed, ao + 2 + OB1)
                        blocks_of(j + 1)
                        input_mats(j + 1)
                    split_lo(h, 2)
                    if not last:
                        dve.drain()
                        dve.wait_ge(y_psum, b + 1)
                        output_mats(j + 1)
                        skips(j + 1)
                        add_skip(b + 1)

                with dve.Fori(0, 3) as j:
                    s5_chunk(l * 4 + j, hl_ + OB1 // 2 + j, j, False)
                s5_chunk(l * 4 + 3, hl_ + OB1 // 2 + 3, 3, True)

                dve.wait_ge(y_psum, l * 4 + 4)
                dve.wait_ge(act_out_freed, ao + 2 + (OB1 + 7))
                src = upool
                for k in range(4):
                    w, dst = 1 << k, (pla, plb)[k % 2]
                    tt(dst[:, k:4, w:S], src[:, k:4, w:S], src[:, k:4, 0:S - w], ADD)
                    dve.tensor_copy(dst[:, k:4, 0:w], src[:, k:4, 0:w])
                    dve.drain()
                    src = dst
                for g in range(4):
                    w = 2 << g
                    v = (pla, plb)[g % 2][:, g, :]
                    ic = cnv("icnt")[:, 16 * g:16 * g + w]
                    tt(v[:, 0:w], v[:, 0:w], ic, MUL)
                    dve.scalar_tensor_tensor(v[:, w:S], v[:, w:S], 1.0 / w, upool[:, g, w:S], MUL, SUB)
                    dve.drain()
                    x = tt(v[:, 0:w], v[:, 0:w], upool[:, g, 0:w], SUB)
                x.then_inc(pool_ready, 1)
                with dve.Fori(0, 4) as j:
                    b = l * 4 + j
                    h = hl_ + OB2 // 2 + j * 2
                    split_lo(h, 1)
                    split_lo(h, 2)
                    dve.wait_ge(q_rot_psum, b + 1)
                    tt(qt1[:, :], qraw[:, :], cos_t[:, :], MUL)
                    tt(qt2[:, :], ps[:, 6, :], sin_t[:, :], MUL)
                    dve.drain()
                    tt(qro[:, :], qt1[:, :], qt2[:, :], ADD).then_inc(q_ready, 1)
                    dve.wait_ge(yfm_in, (l + 1) * 64)
                    gelu(yfm[:, ds(j, 1), :].rearrange("p a n -> p (a n)"), ygt[:, :], l * 5 + j + 1).then_inc(ygelu_ready, 1)
                    split_lo(h, 3)
                    dve.wait_ge(ys_hi, b + 1)
                    o = ysl[:, ds(j, 1), :].rearrange("p a (n t) -> p (a n) t", t=TAP)
                    dve.scalar_tensor_tensor(o, ygt[:, :].rearrange("p (t n) -> p n t", n=NCH), 0.5,
                                             ysh[:, ds(j, 1), :].rearrange("p a (n t) -> p (a n) t", t=TAP).bitcast(f32), MUL, SUB).then_inc(ys_ready, 1)
                    def max_part(s):
                        t = s % 4
                        dve.wait_ge(s_psum, b * 8 + (s + 1))
                        dve.tensor_reduce(tiny[:, 28 + 8 * (s % 3):30 + 8 * (s % 3)], ps[:, sbank(s):sbank(s) + 2, 0:P * (t + 1)], AX.X, MAX,
                                          negate=True).then_inc(s_max, 1)

                    dve.wait_ge(cs_psum, b + 1)
                    c2 = pc[:, :, :].rearrange("p (v t) n -> p v (t n)", v=2)
                    mc, sc, al = tiny[:, 0:8], tiny[:, 8:16], tiny[:, 16:24]
                    tt(c2, ps[:, 2:4, 0:4 * NCMP], bc(cnv("cadd"), 1, 2), ADD)
                    dve.drain()
                    dve.tensor_reduce(mc, pc[:, :, :], AX.X, MAX)
                    dve.drain()
                    tt(pc[:, :, :], pc[:, :, :], bc(mc, 2, NCMP), SUB).then_inc(cs_shift, 1)

                    max_part(0)
                    dve.wait_ge(cs_exp, b + 1)
                    dve.tensor_reduce(sc, pc[:, :, :], AX.X, ADD)
                    dve.drain()
                    dve.reciprocal(sc, sc)
                    dve.drain()
                    for kv in range(2):
                        tt(al[:, 4 * kv:4 * kv + 4], sc[:, 4 * kv:4 * kv + 4], gq[:, :, ds(j * 6 + 3 * kv, 1)].rearrange("p t a -> p (t a)"), MUL)
                    dve.drain()
                    tt(pc[:, :, :], pc[:, :, :], bc(al, 2, NCMP), MUL)
                    dve.drain()
                    tt(c2, c2, bc(cnv("c01"), 1, 2), MUL).then_inc(cs_ready, 1)

                    def scale(s):
                        kv, t = s // 4, s % 4
                        n = P * (t + 1)
                        sums, rat = tiny[:, 30 + 8 * (s % 3):32 + 8 * (s % 3)], tiny[:, 52 + 2 * (s % 3):54 + 2 * (s % 3)]
                        dve.wait_ge(s_exp, b * 8 + (s + 1))
                        dve.reciprocal(rat, sums)
                        dve.drain()
                        tt(rat, rat, gq[:, t, ds(j * 6 + (3 * kv + 1), 2)], MUL).then_inc(s_ratio, 1)
                        dve.drain()
                        dve.tensor_scalar(prob[:, s % 3, 1, 0:n], prob[:, s % 3, 1, 0:n], rat[:, 1:2], None, MUL).then_inc(p_win, 1)

                    max_part(1)
                    scale(0)
                    split_lo(h, 4)
                    max_part(2)
                    for s in range(8):
                        n = P * (s % 4 + 1)
                        if s < 7:
                            scale(s + 1)
                        dve.wait_ge(s_tpsum, b * 8 + (s + 1))
                        dve.tensor_copy(probt[:, s % 2, 1, 0:n], ps[:, 3, 0:n]).then_inc(pt_win, 1)
                        if s < 5:
                            max_part(s + 3)
                    dve.wait_ge(o_hi, b + 1)
                    tt(nsl[:, ds(j, 1), :].rearrange("p a n -> p (a n)"), ps[:, 7, :],
                       nsh[:, ds(j, 1), :].rearrange("p a n -> p (a n)").bitcast(f32), SUB).then_inc(o_ready, 1)

                for g in range(4):
                    dve.wait_ge(mix_hi, l * 4 + (g + 1))
                    dve.scalar_tensor_tensor(pll[:, g, :], ps[:, 4 + g, :], smv("psc")[:, g:g + 1], plh[:, g, :].bitcast(f32), MUL, SUB)\
                       .then_inc(mix_ready, 1)
                with dve.Fori(0, NGL // 2) as i:
                    h = hl_ + OGL // 2 + i
                    for c in range(2):
                        split_lo(h, c + 1)
                        dve.wait_ge(glu_tanh, l * 4 + i * 2 + (c + 1))
                        dve.scalar_tensor_tensor(gv[:, :], gt[:, :], 1.0, ps[:, 2 * c, :], ADD, MUL).then_inc(glu_raw, 1)
                        dve.wait_ge(glu_hi, l * 4 + i * 2 + (c + 1))
                        o = ds(i * 2 + c, 1)
                        dve.scalar_tensor_tensor(gll[:, o, :].rearrange("p a n -> p (a n)"), gv[:, :], 0.5,
                                                 glh[:, o, :].rearrange("p a n -> p (a n)").bitcast(f32), MUL, SUB).then_inc(glu_ready, 1)
                        dve.drain()
                        dve.memset(tiny[:, 0:1], 0.0).then_inc(dve_out_freed, 2)
                with dve.Fori(0, 2) as i:
                    h = hl_ + OC // 2 + i * 5

                    def low_parts(pr):
                        dve.wait_ge(mg_hi, l * 4 + i * 2 + (pr + 1))
                        o = ds(i * 4 + 2 * pr, 2)
                        dve.scalar_tensor_tensor(mgl[:, o, :], acc[:, :, :], 0.5, mgh[:, o, :].bitcast(f32), MUL, SUB).then_inc(mg_ready, 1)

                    for c in range(10):
                        split_lo(h, c + 1)
                        if c == 5:
                            low_parts(0)
                        q, pr = c % 5, c // 5
                        flat = "p b n -> p (b n)"
                        if q in (0, 1):
                            dst = (acc, tmp)[q]
                            dve.drain()
                            slab_out(h, c)
                            dve.scalar_tensor_tensor(dst[:, :, :].rearrange(flat), gates[:, ds(i * 4 + (2 * pr + 8 * q), 2), :].rearrange(flat), 1.0,
                                                     ps[:, 2 * q:2 * q + 2, :].rearrange(flat), ADD, MUL).then_inc(dve_out_freed, 2)
                        if q == 4:
                            slab_out(h, c)
                            dve.wait_ge(mg_tanh, l * 4 + i * 2 + (pr + 2))
                            dve.scalar_tensor_tensor(tmp[:, :, :].rearrange(flat), tg2[:, :, :].rearrange(flat), 1.0,
                                                     ps[:, 2:4, :].rearrange(flat), ADD, MUL).then_inc(dve_out_freed, 4)
                        if q in (1, 4):
                            dve.drain()
                            x = tt(acc[:, :, :], acc[:, :, :], tmp[:, :, :], ADD)
                            dve.drain()
                        if q == 4:
                            x.then_inc(mg_raw, 1)
                    low_parts(1)
                for c in range(NO):
                    split_lo(hl_ + OO // 2, c + 1)
                    slab_out(hl_ + OO // 2, c)
                    residual(r1[:, c, :], c, c % 4, c)
                    if c:
                        stats(c - 1, 4 + (c - 1) % 2, l * 16 + (c - 1))
                stats(NO - 1, 5, l * 16 + (NO - 1))
                ln_part(r1, l * 2)
                with dve.Fori(0, NF // 4) as i:
                    h = hl_ + OF // 2 + i * 2
                    for c in range(4):
                        split_lo(h, c + 1)
                        p = c // 2
                        if c % 2 == 0:
                            dve.wait_ge(ff_tanh, l * KF + i * 2 + (p + 1))
                            dve.scalar_tensor_tensor(fa[:, p, :], ft[:, p, :], 1.0, ps[:, c, :], ADD, MUL)
                        else:
                            dve.drain()
                            slab_out(h, c)
                            tt(fb[:, p, :], fa[:, p, :], ps[:, c, :], MUL).then_inc(ff_raw, 1)
                            dve.wait_ge(ff_hi, l * KF + i * 2 + (p + 1))
                            o = ds(i * 2 + p, 1)
                            dve.scalar_tensor_tensor(hl[:, o, :].rearrange("p a n -> p (a n)"), fb[:, p, :], 0.5,
                                                     hh[:, o, :].rearrange("p a n -> p (a n)").bitcast(f32), MUL, SUB).then_inc(ff_ready, 1)
                            dve.drain()
                            dve.memset(tiny[:, 0:1], 0.0).then_inc(dve_out_freed, 2)
                def stats_of(n, m, o):
                    dve.wait_ge(rt_psum, n + 1)
                    for t in range(4):
                        x = dve.bn_stats(lnst[:, t, ds(m, 1), :].rearrange("p a s -> p (a s)"), ps[:, 4 + o, P * t:P * t + P])
                    x.then_inc(stats_done, 1)

                def two_outputs(i, first=False):
                    h = hl_ + OG // 2 + i * 3
                    for o in range(2):
                        split_lo(h, 3 * o + 1)
                        if o == 1:
                            stats_of(l * 16 + 8 + i * 2, i * 2, 0)
                        elif not first:
                            stats_of(l * 16 + 7 + i * 2, i * 2 - 1, 1)
                        split_lo(h, 3 * o + 2)
                        split_lo(h, 3 * o + 3)
                        if not first:
                            dve.wait_ge(r_kept, l * 8 + i * 2 + (o - 1))
                        slab_out(h, 3 * o + 2)
                        m1 = ds(i * 2 + o, 1)
                        flat = "p a n -> p (a n)"
                        dve.scalar_tensor_tensor(rst[:, o, :], xh[:, m1, :].rearrange(flat).bitcast(f32), ALPHA, ps[:, o, :], MUL, ADD).then_inc(dve_out_freed, 1)
                        dve.drain()
                        dve.scalar_tensor_tensor(rst[:, o, :], xl[:, m1, :].rearrange(flat).bitcast(f32), ALPHA, rst[:, o, :], MUL, ADD).then_inc(r_ready, 1)

                two_outputs(0, True)
                with dve.Fori(0, 3) as i:
                    two_outputs(i + 1)
                dve.wait_ge(r_kept, l * 8 + 8)
                stats_of(l * 16 + 15, 7, 1)
                ln_part(xf, l * 2 + 1)


def packed(v):
    f = np.float32
    w_in, w_br = v["w_in"], v["w_branch"]
    heads = np.concatenate([np.r_[h * HD:(h + 1) * HD] for j in range(4) for h in (j, j + 4)])
    stream = np.zeros((L, NSLAB, P, 8, P), f)

    def chunks(w, cols):
        return w[:, cols].reshape(-1, P, len(cols)).transpose(1, 0, 2)

    for l in range(L):
        n = 0

        def put(*parts):
            nonlocal n
            at = 0
            for part in parts:
                stream[l, n, :, at:at + part.shape[1], :] = part
                at += part.shape[1]
            n += 1

        def cols(a):
            return np.arange(a, a + P)

        for a in (1792, 2048, 1536, 1664, 1920, 2176):
            put(chunks(w_in[l], cols(a)))
        for j in range(4):
            put(chunks(w_in[l], cols(P * j)))
        gate0 = 2328
        for j in range(4):
            put(chunks(w_in[l], cols(512 + P * j)))
            put(chunks(w_in[l], cols(gate0 + P * j)))
        for j in range(4):
            put(chunks(w_in[l], 1024 + heads[P * j:P * j + P]))
            for c in range(3):
                put(chunks(w_in[l], cols(gate0 + P * (4 + 3 * j + c))))
        for m in range(4):
            put(chunks(v["ssm_w_glu"][l], cols(P * m)), chunks(v["ssm_w_glu"][l], cols(512 + P * m)))
        br = [w_br[l, 0], w_br[l, 1], w_br[l, 2][heads]]
        for m in range(0, 8, 2):
            for b in (0, 1):
                put(chunks(br[b], cols(P * m)), chunks(br[b], cols(P * (m + 1))))
            for c in (0, 1):
                put(chunks(w_in[l], cols(gate0 + P * (16 + m + c))))
            put(chunks(br[2], cols(P * m)), chunks(br[2], cols(P * (m + 1))))
        for m in range(8):
            put(chunks(v["w_out"][l], cols(P * m)))
        for i in range(KF):
            put(chunks(v["ffn_w_in"][l], cols(P * i)))
            put(chunks(v["ffn_w_in"][l], cols(FF + P * i)))
        for m in range(8):
            w = chunks(v["ffn_w_out"][l], cols(P * m))
            for q in range(3):
                put(w[:, 8 * q:8 * q + 8])
        assert n == NSLAB
    w1s = v["cmp_w1"].reshape(L * 2, 16, P, CH).transpose(0, 2, 1, 3).reshape(L * 2, P, 16 * CH)
    sm = np.zeros((L, P, NSM), f)

    def fill(name, x):
        a, b = SM[name]
        sm[:, :, a:b] = x.reshape(L, P, b - a)

    def by_state(x):
        return np.moveaxis(x.reshape(L, GP, 2 * SN, *x.shape[3:]), 1, 2)

    fill("are", by_state(v["ssm_a_re"]))
    fill("aim", by_state(v["ssm_a_im"]))
    fill("ldt", by_state(np.broadcast_to(v["ssm_log_dt"][:, :, None], (L, SG, SN))))
    fill("bre", by_state(v["ssm_b_re"]))
    fill("bim", by_state(v["ssm_b_im"]))
    fill("cre", by_state(v["ssm_c_re"].transpose(0, 1, 3, 2)))
    fill("cim", by_state(v["ssm_c_im"].transpose(0, 1, 3, 2)))
    dsk = np.zeros((L, P, SG), f)
    dsk[:, 0:SC, :] = v["ssm_d"].reshape(L, SG, SC).transpose(0, 2, 1)
    fill("dsk", dsk)
    fill("psc", v["pool_scale"].reshape(L, 4, P).transpose(0, 2, 1))
    fill("b1", v["cmp_b1"].reshape(L, 4, P).transpose(0, 2, 1))
    g24 = [2304 + b * 8 + kv * 4 + j for j in range(4) for kv in range(2) for b in range(3)]
    fill("wg", v["w_in"][:, :, g24].reshape(L, KD, P, 24).transpose(0, 2, 1, 3))
    fill("wpool", v["pool_w"].transpose(0, 2, 1, 3))
    fill("w2", v["cmp_w2"].reshape(L, 4, P, HD).transpose(0, 2, 1, 3))
    fill("pos", v["cmp_pos"].reshape(L, 2, 16, P).transpose(0, 3, 1, 2))
    norms = np.zeros((P, L, 32), f)
    for w in range(2):
        norms[:, :, 16 * w:16 * w + 8] = v["ln_g"][:, w].reshape(L, KD, P).transpose(2, 0, 1)
        norms[:, :, 16 * w + 8:16 * w + 16] = v["ln_b"][:, w].reshape(L, KD, P).transpose(2, 0, 1)
    cn = np.zeros((P, NCN), f)
    i = np.arange(P)

    def const(name, x):
        a, b = CN[name]
        cn[:, a:b] = x.reshape(P, b - a)

    const("ident", np.eye(P, dtype=f))
    rot = np.zeros((P, P), f)
    for m in range(P):
        if m % HD < HD // 2:
            rot[m + HD // 2, m] = -1.0
        else:
            rot[m - HD // 2, m] = 1.0
    const("rot", rot)
    const("dmask", np.where(i[None, :] > i[:, None], NEG, 0.0).astype(f))
    tok = np.arange(4)[None, :, None] * P + i[:, None, None]
    seen = CSTR * np.arange(NCMP)[None, None, :] + 31 <= tok
    const("cadd", np.where(seen, 0.0, NEG).astype(f))
    const("c01", seen.astype(f))
    icnt = np.zeros((4, 16), f)
    for g in range(4):
        icnt[g] = 1.0 / np.minimum(np.arange(16) + 1, 2 << g)
    const("icnt", np.broadcast_to(icnt.reshape(1, 64), (P, 64)))
    inv = np.power(f(10000.0), -np.arange(0, HD, 2, dtype=f) / f(HD)).astype(f)
    const("inv", np.tile(inv, 4))
    xin = v["x"][0].T.reshape(KD, P, S).transpose(1, 0, 2)
    return {"wstream": stream.reshape(L * NSLAB, P, 1024), "w1s": w1s, "smalls": sm, "norms": norms, "consts": cn,
            "xin": xin, "pos": v["positions"].astype(np.int32)}


def kernel(**inputs):
    import concourse.bacc as bacc
    from concourse.bass_utils import run_bass_kernel_spmd

    arrays = {k: np.ascontiguousarray(a) for k, a in packed({k: np.asarray(a) for k, a in inputs.items()}).items()}
    nc = bacc.Bacc("TRN2", target_bir_lowering=False, num_devices=1)
    args = {k: nc.dram_tensor(k, a.shape, mybir.dt.from_np(a.dtype), kind="ExternalInput").ap() for k, a in arrays.items()}
    out = nc.dram_tensor("out", (P, KD, S), mybir.dt.float32, kind="ExternalOutput").ap()
    build_program(nc, out=out, **args)
    r = run_bass_kernel_spmd(nc, [arrays], core_ids=[0])
    y = r.results[0]["out"]
    return np.ascontiguousarray(y.transpose(1, 0, 2).reshape(D, S).T)[None]
```
